# Optimizing a Trainium2 kernel written in Bass

```python
import jax, jax.numpy as jnp
from jax import lax
import numpy as np

D_MODEL = 1024
BATCH = 1
SEQ = 2048
DEPTH = 1

D_MIX = D_MODEL
HEAD_DIM = 64
N_ATTN_HEADS = 8
ATTN_DIM = N_ATTN_HEADS * HEAD_DIM
N_CONV_GROUPS = 8
CONV_DIM = D_MIX - ATTN_DIM
CONV_WIDTH = 3
IN_COLS = 3 * ATTN_DIM + 3 * CONV_DIM
D_FF = ((8 * D_MODEL // 3 + 255) // 256) * 256
Q_BLOCK = 128
EPS = 1e-6

kernel_name = "hymba_stickbreak_shortconv_swiglu"

def _rms_norm(x, gain):
    x32 = x.astype(jnp.float32)
    y = x32 * lax.rsqrt(jnp.mean(x32 * x32, axis=-1, keepdims=True) + EPS)
    return (y * gain.astype(jnp.float32)).astype(x.dtype)

def _stick_breaking_attention(q, k, v):
    b, h, s, dh = q.shape
    nb = s // Q_BLOCK
    scale = dh ** -0.5
    k32 = k.astype(jnp.float32)
    v32 = v.astype(jnp.float32)
    q_blocks = q.reshape(b, h, nb, Q_BLOCK, dh).transpose(2, 0, 1, 3, 4)
    starts = jnp.arange(nb, dtype=jnp.int32) * Q_BLOCK
    key_pos = jnp.arange(s, dtype=jnp.int32)

    def one_block(args):
        q_blk, start = args
        z = jnp.einsum('bhqd,bhkd->bhqk', q_blk.astype(jnp.float32), k32) * scale
        q_pos = start + jnp.arange(Q_BLOCK, dtype=jnp.int32)
        causal = key_pos[None, :] < q_pos[:, None]
        sp = jax.nn.softplus(z)
        neg_log_rem = jnp.where(causal, sp, 0.0)
        after = lax.cumsum(neg_log_rem, axis=3, reverse=True) - neg_log_rem
        log_a = (z - sp) - after
        a = jnp.where(causal, jnp.exp(log_a), 0.0)
        return jnp.einsum('bhqk,bhkd->bhqd', a, v32)

    out = lax.map(one_block, (q_blocks, starts))
    return out.transpose(1, 2, 0, 3, 4).reshape(b, h, s, dh).astype(q.dtype)

def _short_conv_mixer(b_gate, c_gate, u, conv_w):
    h = c_gate * u
    rhs = conv_w.astype(h.dtype)[:, None, :]
    y = lax.conv_general_dilated(h, rhs, window_strides=(1,), padding=[(CONV_WIDTH - 1, 0)],
                                 dimension_numbers=('NWC', 'WIO', 'NWC'),
                                 feature_group_count=CONV_DIM)
    return b_gate * y

def setup_inputs(seed: int = 0) -> dict:
    key = jax.random.key(seed)
    ks = jax.random.split(key, 12)
    f32 = jnp.float32

    def gain(k, shape):
        return jnp.ones(shape, f32) + 0.01 * jax.random.normal(k, shape, f32)

    x = jax.random.normal(ks[0], (BATCH, SEQ, D_MODEL), f32)
    norm_mix = gain(ks[1], (DEPTH, D_MODEL))
    w_in = jax.random.normal(ks[2], (DEPTH, D_MODEL, IN_COLS), f32) * D_MODEL ** -0.5
    q_norm = gain(ks[3], (DEPTH, HEAD_DIM))
    k_norm = gain(ks[4], (DEPTH, HEAD_DIM))
    conv_w = jax.random.normal(ks[5], (DEPTH, CONV_WIDTH, CONV_DIM), f32) * CONV_WIDTH ** -0.5
    w_out = jax.random.normal(ks[6], (DEPTH, D_MIX, D_MODEL), f32) * D_MIX ** -0.5
    norm_ffn = gain(ks[7], (DEPTH, D_MODEL))
    w_gate = jax.random.normal(ks[8], (DEPTH, D_MODEL, D_FF), f32) * D_MODEL ** -0.5
    w_up = jax.random.normal(ks[9], (DEPTH, D_MODEL, D_FF), f32) * D_MODEL ** -0.5
    w_down = jax.random.normal(ks[10], (DEPTH, D_FF, D_MODEL), f32) * D_FF ** -0.5
    return {"x": x, "norm_mix": norm_mix, "w_in": w_in, "q_norm": q_norm, "k_norm": k_norm,
            "conv_w": conv_w, "w_out": w_out, "norm_ffn": norm_ffn, "w_gate": w_gate,
            "w_up": w_up, "w_down": w_down}

def reference(x, norm_mix, w_in, q_norm, k_norm, conv_w, w_out, norm_ffn, w_gate, w_up, w_down):
    b, s, _ = x.shape
    splits = [ATTN_DIM, 2 * ATTN_DIM, 3 * ATTN_DIM,
              3 * ATTN_DIM + CONV_DIM, 3 * ATTN_DIM + 2 * CONV_DIM]
    for l in range(DEPTH):
        h = _rms_norm(x, norm_mix[l])
        proj = h @ w_in[l].astype(h.dtype)
        q, k, v, cb, cc, cu = jnp.split(proj, splits, axis=-1)
        q = _rms_norm(q.reshape(b, s, N_ATTN_HEADS, HEAD_DIM), q_norm[l])
        k = _rms_norm(k.reshape(b, s, N_ATTN_HEADS, HEAD_DIM), k_norm[l])
        v = v.reshape(b, s, N_ATTN_HEADS, HEAD_DIM)
        attn = _stick_breaking_attention(q.transpose(0, 2, 1, 3), k.transpose(0, 2, 1, 3),
                                         v.transpose(0, 2, 1, 3))
        attn = attn.transpose(0, 2, 1, 3).reshape(b, s, ATTN_DIM)
        conv = _short_conv_mixer(cb, cc, cu, conv_w[l])
        mix = jnp.concatenate([attn, conv], axis=-1)
        x = x + mix @ w_out[l].astype(mix.dtype)
        h = _rms_norm(x, norm_ffn[l])
        g = h @ w_gate[l].astype(h.dtype)
        u = h @ w_up[l].astype(h.dtype)
        x = x + (jax.nn.silu(g) * u) @ w_down[l].astype(h.dtype)
    return x


_drawn_inputs = setup_inputs


def setup_inputs(seed=0):
    import zlib

    import numpy as np

    out = dict(_drawn_inputs(seed))
    spreads = {}
    factors = {'norm_mix': 4.696, 'q_norm': 8.0, 'k_norm': 8.0, 'norm_ffn': 8.0}
    for name, (base, spread) in spreads.items():
        noise = np.random.default_rng([zlib.crc32(name.encode()), seed]).standard_normal(out[name].shape)
        drawn = base * np.exp(spread * noise) if base else spread * noise
        out[name] = __import__('jax').numpy.asarray(drawn.astype(out[name].dtype))
    for name, factor in factors.items():
        out[name] = (out[name] * factor).astype(out[name].dtype)
    return out
```

```python
from contextlib import ExitStack

import concourse.bass as bass
from concourse import mybir

F32 = mybir.dt.float32
F32R = mybir.dt.float32r
BF16 = mybir.dt.bfloat16
ACT = mybir.ActivationFunctionType
ALU = mybir.AluOpType
AX = mybir.AxisListType

P = 128
BANK = 512
EPS = 1e-6
MASKED = -1e30
DMA = 16


def wait(eng, sem, value):
    if not isinstance(value, int) or value > 0:
        eng.wait_ge(sem, value)


class Pool_:

    def __init__(self, nc, stack, prefix):
        self.nc, self.stack, self.prefix = nc, stack, prefix

    def sb(self, name, shape, dt=F32):
        return self.stack.enter_context(self.nc.sbuf_tensor(self.prefix + name, shape, dt))

    def ps(self, name, shape, dt=F32):
        return self.stack.enter_context(self.nc.psum_tensor(self.prefix + name, shape, dt))

    def sem(self, name):
        return self.stack.enter_context(self.nc.semaphore(self.prefix + name))

    def block(self):
        return self.stack.enter_context(self.nc.Block())


def matmul3(nc, out, lhs_hi, lhs_lo, rhs_hi, rhs_lo, first, last):
    nc.tensor.matmul(out, lhs_hi, rhs_hi, start=first, stop=False)
    nc.tensor.matmul(out, lhs_hi, rhs_lo, start=False, stop=False)
    return nc.tensor.matmul(out, lhs_lo, rhs_hi, start=False, stop=last)


def constants(nc, cst):
    with ExitStack() as stack:
        m = Pool_(nc, stack, "cst_")
        filled, picked, copied = m.sem("filled"), m.sem("picked"), m.sem("copied")
        mask32 = m.sb("mask32", [P, P])
        block = m.block()

        @block.gpsimd
        def _(pool):
            nc.gpsimd.memset(cst["ident"][:, :], 0.0).then_inc(filled, 1)
            nc.gpsimd.memset(mask32[:, :], 0.0).then_inc(filled, 1)
            nc.gpsimd.memset(cst["minus_half"][:, :], -0.5).then_inc(filled, 1)
            nc.gpsimd.memset(cst["eps"][:, :], EPS).then_inc(filled, 1)
            pool.wait_ge(filled, 4)
            nc.gpsimd.affine_select(out=cst["ident"][:, :], in_=cst["ident"][:, :], compare_op=ALU.not_equal,
                                    fill=1.0, base=0, pattern=[[-1, P]], channel_multiplier=1).then_inc(picked, 1)
            nc.gpsimd.affine_select(out=mask32[:, :], in_=mask32[:, :], compare_op=ALU.is_gt,
                                    fill=MASKED, base=0, pattern=[[-1, P]], channel_multiplier=1).then_inc(picked, 1)

        @block.vector
        def _(dve):
            dve.wait_ge(picked, 2)
            nc.vector.tensor_copy(cst["ident_bf"][:, :], cst["ident"][:, :]).then_inc(copied, 1)
            nc.vector.tensor_copy(cst["mask_bf"][:, :], mask32[:, :]).then_inc(copied, 1)
            dve.wait_ge(copied, 2)


def qkv_stage(nc, cst, x, norm_mix, w_in, q_norm, k_norm, qk_hi_dram, qk_lo_dram, v_dram):
    S, D = x.shape
    KT = D // P
    TILES = S // P
    AD = v_dram.shape[1]
    HD = q_norm.shape[0]
    HEADS = AD // HD
    PAIRS = AD // P
    COLS = 3 * AD
    NB = KT // 4
    with ExitStack() as stack:
        m = Pool_(nc, stack, "qkv_")
        w_stage = m.sb("w_stage", [P, 2, COLS])
        w_hi, w_lo = m.sb("w_hi", [P, KT, COLS], F32R), m.sb("w_lo", [P, KT, COLS], F32R)
        gain = m.sb("gain", [P, D])
        qk_gain = m.sb("qk_gain", [P, 2])
        x_t = m.sb("x_t", [P, 2, D])
        square = m.sb("square", [P, D])
        ss, msq, rstd = m.sb("ss", [P, 2]), m.sb("msq", [P, 2]), m.sb("rstd", [P, 2])
        xn = m.sb("xn", [P, 2, D])
        hT_hi, hT_lo = m.sb("hT_hi", [P, 2, KT, P], F32R), m.sb("hT_lo", [P, 2, KT, P], F32R)
        qk_square = m.sb("qk_square", [P, 2 * AD])
        qk_ss, qk_msq, qk_rstd = (m.sb(n, [P, 2 * HEADS]) for n in ("qk_ss", "qk_msq", "qk_rstd"))
        qk_n = m.sb("qk_n", [P, 2 * AD])
        v_out = m.sb("v_out", [P, 2, AD])
        qkT_hi, qkT_lo = m.sb("qkT_hi", [P, 2, 2 * PAIRS, P], F32R), m.sb("qkT_lo", [P, 2, 2 * PAIRS, P], F32R)
        proj = m.ps("proj", [P, 2, 3, BANK])
        tr_x, tr_qk = m.ps("tr_x", [P, 4, P]), m.ps("tr_qk", [P, 4, P])

        gains_in, x_in = m.sem("gains_in"), [m.sem("x_in0"), m.sem("x_in1")]
        w_in_sem = [m.sem("w_in0"), m.sem("w_in1")]
        w_hi_done, w_lo_done = m.sem("w_hi_done"), m.sem("w_lo_done")
        ss_done, msq_done, rstd_done, xn_done = (m.sem(n) for n in ("ss_done", "msq_done", "rstd_done", "xn_done"))
        tx_full, hT_hi_done, hT_lo_done = m.sem("tx_full"), m.sem("hT_hi_done"), m.sem("hT_lo_done")
        proj_full, square_done, v_done = m.sem("proj_full"), m.sem("square_done"), m.sem("v_done")
        qk_ss_done, qk_msq_done, qk_rstd_done, qk_n_done = (
            m.sem(n) for n in ("qk_ss_done", "qk_msq_done", "qk_rstd_done", "qk_n_done"))
        tq_full, qkT_hi_done, qkT_lo_done = m.sem("tq_full"), m.sem("qkT_hi_done"), m.sem("qkT_lo_done")
        v_stored, qkT_stored = [m.sem("v_stored0"), m.sem("v_stored1")], [m.sem("qkT_stored0"), m.sem("qkT_stored1")]
        block = m.block()

        def tiles(eng, step):
            step(0, 0, first=True)
            step(1, 1)
            step(2, 0)
            with eng.Fori(1, (TILES - 2) // 2) as i:
                step(2 * i + 1, 1)
                step(2 * i + 2, 0)
            step(TILES - 1, (TILES - 1) % 2, last=True)

        @block.sync
        def _(sp):
            sp.dma_start(x_t[:, 0, :], x[0:P, :]).then_inc(x_in[0], DMA)
            sp.dma_start(gain[:, :], norm_mix.partition_broadcast(P)).then_inc(gains_in, DMA)
            for j, g in enumerate((q_norm, k_norm)):
                for half in range(P // HD):
                    sp.dma_start(qk_gain[half * HD:(half + 1) * HD, j:j + 1],
                                 g.rearrange("(p o) -> p o", o=1)).then_inc(gains_in, DMA)
            for k in range(KT):
                wait(sp, w_lo_done, k - 1)
                sp.dma_start(w_stage[:, k % 2, :], w_in[k * P:(k + 1) * P, 0:COLS]).then_inc(w_in_sem[k % 2], DMA)

            def step(t, b, first=False, last=False):
                if not last:
                    wait(sp, xn_done, t)
                    sp.dma_start(x_t[:, 1 - b, :], x[bass.ds((t + 1) * P, P), :]).then_inc(x_in[1 - b], DMA)
                if not first:
                    sp.wait_ge(qkT_lo_done, 2 * t)
                sp.wait_ge(v_done, t + 1)
                sp.dma_start(v_dram[bass.ds(t * P, P), :], v_out[:, b, :]).then_inc(v_stored[b], DMA)
                if not first:
                    store_qk(t - 1, 1 - b)

            def store_qk(t, b):
                for src, dst in ((qkT_hi, qk_hi_dram), (qkT_lo, qk_lo_dram)):
                    sp.dma_start(dst.rearrange("(c p) t -> p c t", p=P)[:, :, bass.ds(t * P, P)],
                                 src[:, b, :, :].bitcast(F32)).then_inc(qkT_stored[b], DMA)

            tiles(sp, step)
            sp.wait_ge(qkT_lo_done, 2 * TILES)
            store_qk(TILES - 1, (TILES - 1) % 2)
            for b in range(2):
                sp.wait_ge(v_stored[b], DMA * TILES // 2)
                sp.wait_ge(qkT_stored[b], DMA * TILES)

        @block.gpsimd
        def _(pool):
            def x_rstd(t, b):
                pool.wait_ge(ss_done, t + 1)
                nc.gpsimd.tensor_tensor(msq[:, b:b + 1], ss[:, b:b + 1], cst["eps"][:, 0:1],
                                        ALU.add).then_inc(msq_done, 1)
                pool.wait_ge(msq_done, t + 1)
                nc.gpsimd.tensor_tensor(rstd[:, b:b + 1], msq[:, b:b + 1], cst["minus_half"][:, 0:1],
                                        ALU.pow).then_inc(rstd_done, 1)

            x_rstd(0, 0)

            def step(t, b, first=False, last=False):
                if not last:
                    x_rstd(t + 1, 1 - b)
                pool.wait_ge(qk_ss_done, t + 1)
                nc.gpsimd.tensor_tensor(qk_msq[:, :], qk_ss[:, :], cst["eps"][:, 0:2 * HEADS],
                                        ALU.add).then_inc(qk_msq_done, 1)
                pool.wait_ge(qk_msq_done, t + 1)
                nc.gpsimd.tensor_tensor(qk_rstd[:, :], qk_msq[:, :], cst["minus_half"][:, 0:2 * HEADS],
                                        ALU.pow).then_inc(qk_rstd_done, 1)

            tiles(pool, step)

        @block.scalar
        def _(act):
            def x_square(t, b):
                act.wait_ge(x_in[b], DMA * (t // 2 + 1) if isinstance(t, int) else x_count(t, b))
                wait(act, ss_done, t)
                nc.scalar.activation(square[:, :], x_t[:, b, :], ACT.Square, scale=D ** -0.5,
                                     accum_out=ss[:, b:b + 1]).then_inc(ss_done, 1)

            def x_count(t, b):
                return (t - b) * (DMA // 2) + DMA

            def hT_part(t, b, n):
                act.wait_ge(tx_full, NB * t + n + 1)
                wait(act, proj_full, 3 * (t - 1))
                nc.scalar.activation(hT_hi[:, b, 4 * n:4 * n + 4, :], tr_x[:, :, :], ACT.Copy).then_inc(hT_hi_done, 1)

            def qkT_part(t, b, n):
                act.wait_ge(tq_full, 2 * t + n + 1)
                wait(act, qkT_stored[b], DMA * (t - b))
                nc.scalar.activation(qkT_hi[:, b, PAIRS * n:PAIRS * (n + 1), :], tr_qk[:, :, :], ACT.Copy,
                                     scale=qk_gain[:, n:n + 1]).then_inc(qkT_hi_done, 1)

            def head_square(t, b, n):
                act.wait_ge(proj_full, 3 * t + n + 1)
                wait(act, qk_ss_done, t)
                nc.scalar.activation(qk_square[:, n * AD:(n + 1) * AD], proj[:, b, n, 0:AD],
                                     ACT.Square, scale=HD ** -0.5).then_inc(square_done, 1)

            x_square(0, 0)
            for k in range(KT):
                act.wait_ge(w_in_sem[k % 2], DMA * (k // 2 + 1))
                nc.scalar.activation(w_hi[:, k, :], w_stage[:, k % 2, :], ACT.Copy).then_inc(w_hi_done, 1)
            act.wait_ge(gains_in, DMA * 5)
            for n in range(NB):
                hT_part(0, 0, n)

            def step(t, b, first=False, last=False):
                if not last:
                    x_square(t + 1, 1 - b)
                head_square(t, b, 0)
                if not first:
                    qkT_part(t - 1, 1 - b, 0)
                if not last:
                    hT_part(t + 1, 1 - b, 0)
                head_square(t, b, 1)
                if not first:
                    qkT_part(t - 1, 1 - b, 1)
                if not last:
                    hT_part(t + 1, 1 - b, 1)
                act.wait_ge(proj_full, 3 * t + 3)
                wait(act, v_stored[b], (DMA // 2) * (t - b))
                nc.scalar.activation(v_out[:, b, :], proj[:, b, 2, 0:AD], ACT.Copy).then_inc(v_done, 1)

            tiles(act, step)
            for n in range(2):
                qkT_part(TILES - 1, (TILES - 1) % 2, n)

        @block.vector
        def _(dve):
            def x_norm(t, b):
                dve.wait_ge(rstd_done, t + 1)
                wait(dve, tx_full, NB * (t - 1))
                nc.vector.scalar_tensor_tensor(out=xn[:, b, :], in0=x_t[:, b, :], scalar=rstd[:, b:b + 1],
                                               in1=gain[:, :], op0=ALU.mult, op1=ALU.mult).then_inc(xn_done, 1)

            def hT_part(t, b, n):
                dve.wait_ge(hT_hi_done, NB * t + n + 1)
                nc.vector.tensor_tensor(hT_lo[:, b, 4 * n:4 * n + 4, :], tr_x[:, :, :],
                                        hT_hi[:, b, 4 * n:4 * n + 4, :].bitcast(F32),
                                        ALU.subtract).then_inc(hT_lo_done, 1)

            def qkT_part(t, b, n):
                dve.wait_ge(qkT_hi_done, 2 * t + n + 1)
                nc.vector.scalar_tensor_tensor(out=qkT_lo[:, b, PAIRS * n:PAIRS * (n + 1), :], in0=tr_qk[:, :, :],
                                               scalar=qk_gain[:, n:n + 1],
                                               in1=qkT_hi[:, b, PAIRS * n:PAIRS * (n + 1), :].bitcast(F32),
                                               op0=ALU.mult, op1=ALU.subtract).then_inc(qkT_lo_done, 1)

            dve.wait_ge(gains_in, DMA * 5)
            x_norm(0, 0)
            for k in range(KT):
                dve.wait_ge(w_hi_done, k + 1)
                nc.vector.tensor_tensor(w_lo[:, k, :], w_stage[:, k % 2, :], w_hi[:, k, :].bitcast(F32),
                                        ALU.subtract).then_inc(w_lo_done, 1)
            for n in range(NB):
                hT_part(0, 0, n)

            def step(t, b, first=False, last=False):
                if not last:
                    x_norm(t + 1, 1 - b)
                if not first:
                    qkT_part(t - 1, 1 - b, 0)
                if not last:
                    hT_part(t + 1, 1 - b, 0)
                dve.wait_ge(square_done, 2 * t + 2)
                wait(dve, qk_rstd_done, t)
                nc.vector.reduce_sum(qk_ss[:, :], qk_square[:, :].rearrange("p (h d) -> p h d", d=HD),
                                     axis=AX.X).then_inc(qk_ss_done, 1)
                if not first:
                    qkT_part(t - 1, 1 - b, 1)
                if not last:
                    hT_part(t + 1, 1 - b, 1)
                dve.wait_ge(qk_rstd_done, t + 1)
                wait(dve, tq_full, 2 * t)
                for n in range(2):
                    nc.vector.tensor_tensor(
                        qk_n[:, n * AD:(n + 1) * AD].rearrange("p (h d) -> p h d", d=HD),
                        proj[:, b, n, 0:AD].rearrange("p (h d) -> p h d", d=HD),
                        qk_rstd[:, n * HEADS:(n + 1) * HEADS].unsqueeze(2).to_broadcast([P, HEADS, HD]),
                        ALU.mult).then_inc(qk_n_done, 1)

            tiles(dve, step)
            for n in range(2):
                qkT_part(TILES - 1, (TILES - 1) % 2, n)

        @block.tensor
        def _(pe):
            def x_transpose(t, b, n):
                pe.wait_ge(xn_done, t + 1)
                wait(pe, hT_lo_done, NB * t + n)
                for j in range(4):
                    k = 4 * n + j
                    last = nc.tensor.transpose(tr_x[:, j, :], xn[:, b, k * P:(k + 1) * P], cst["ident"][:, :])
                last.then_inc(tx_full, 1)

            def qk_transpose(t, b, n):
                pe.wait_ge(qk_n_done, 2 * t + n + 1)
                wait(pe, qkT_lo_done, 2 * t + n)
                for j in range(PAIRS):
                    c = n * AD + j * P
                    last = nc.tensor.transpose(tr_qk[:, j, :], qk_n[:, c:c + P], cst["ident"][:, :])
                last.then_inc(tq_full, 1)

            def project(t, b, n):
                if n < 2:
                    wait(pe, qk_n_done, 2 * (t - 1))
                else:
                    wait(pe, v_done, t - 1)
                pe.wait_ge(hT_lo_done, NB * t + NB)
                for k in range(KT):
                    last = matmul3(nc, proj[:, b, n, 0:AD], hT_hi[:, b, k, :], hT_lo[:, b, k, :],
                                   w_hi[:, k, n * AD:(n + 1) * AD], w_lo[:, k, n * AD:(n + 1) * AD],
                                   k == 0, k == KT - 1)
                last.then_inc(proj_full, 1)

            for n in range(NB):
                x_transpose(0, 0, n)
            pe.wait_ge(w_lo_done, KT)

            def step(t, b, first=False, last=False):
                project(t, b, 0)
                if not first:
                    qk_transpose(t - 1, 1 - b, 0)
                if not last:
                    x_transpose(t + 1, 1 - b, 0)
                project(t, b, 1)
                if not first:
                    qk_transpose(t - 1, 1 - b, 1)
                if not last:
                    x_transpose(t + 1, 1 - b, 1)
                project(t, b, 2)

            tiles(pe, step)
            for n in range(2):
                qk_transpose(TILES - 1, (TILES - 1) % 2, n)


def conv_stage(nc, cst, x, norm_mix, w_in, conv_w, mixT_dram):
    S, D = x.shape
    KT = D // P
    GROUPS = S // BANK
    GT = BANK // P
    TAPS, CD = conv_w.shape
    COL0 = w_in.shape[1] - 3 * CD
    COLS = 3 * CD
    CT = CD // P
    assert CT == GT
    NB = KT // 4
    with ExitStack() as stack:
        m = Pool_(nc, stack, "conv_")
        w_stage = m.sb("w_stage", [P, 2, COLS])
        w_hi, w_lo = m.sb("w_hi", [P, KT, COLS], F32R), m.sb("w_lo", [P, KT, COLS], F32R)
        gain = m.sb("gain", [P, D])
        taps = m.sb("taps", [P, CT, TAPS])
        x_t = m.sb("x_t", [P, 2, D])
        square = m.sb("square", [P, D])
        ss, msq, rstd = m.sb("ss", [P, 2]), m.sb("msq", [P, 2]), m.sb("rstd", [P, 2])
        xn = m.sb("xn", [P, GT, D])
        hT_hi, hT_lo = m.sb("hT_hi", [P, KT, BANK], F32R), m.sb("hT_lo", [P, KT, BANK], F32R)
        u_sb = m.sb("u_sb", [P, BANK])
        HALO = TAPS - 1
        cu = m.sb("cu", [P, CT, HALO + BANK])
        conv = m.sb("conv", [P, BANK])
        y = m.sb("y", [P, 2, BANK])
        proj = m.ps("proj", [P, 2, 3, BANK])
        tr = m.ps("tr", [P, 2, 4, P])

        gains_in, x_in = m.sem("gains_in"), [m.sem("x_in0"), m.sem("x_in1")]
        w_in_sem = [m.sem("w_in0"), m.sem("w_in1")]
        w_hi_done, w_lo_done = m.sem("w_hi_done"), m.sem("w_lo_done")
        ss_done, msq_done, rstd_done, xn_done = (m.sem(n) for n in ("ss_done", "msq_done", "rstd_done", "xn_done"))
        tx_full, hT_hi_done, hT_lo_done = m.sem("tx_full"), m.sem("hT_hi_done"), m.sem("hT_lo_done")
        proj_full, u_done, y_done, conv_chain, y_stored0 = (
            m.sem(n) for n in ("proj_full", "u_done", "y_done", "conv_chain", "y_stored0"))
        y_stored = [y_stored0, m.sem("y_stored1")]
        block = m.block()

        def groups(eng, body):
            with eng.Fori(0, GROUPS - 1) as g:
                body(g, True)
            body(GROUPS - 1, False)

        @block.sync
        def _(sp):
            sp.dma_start(gain[:, :], norm_mix.partition_broadcast(P)).then_inc(gains_in, DMA)
            with nc.allow_non_contiguous_dma(reason="conv weights, once"):
                for c in range(CT):
                    sp.dma_start(taps[:, c, :], conv_w[:, c * P:(c + 1) * P].rearrange("w p -> p w")
                                 ).then_inc(gains_in, DMA)

            def load(t, b):
                wait(sp, xn_done, t - 1)
                sp.dma_start(x_t[:, b, :], x[bass.ds(t * P, P), :]).then_inc(x_in[b], DMA)

            for t in range(GT):
                load(t, t % 2)
            for k in range(KT):
                wait(sp, w_lo_done, k - 1)
                sp.dma_start(w_stage[:, k % 2, :],
                             w_in[k * P:(k + 1) * P, COL0:COL0 + COLS]).then_inc(w_in_sem[k % 2], DMA)

            def body(g, more):
                for c in range(CT):
                    if more:
                        load(g * GT + GT + c, c % 2)
                    sp.wait_ge(y_done, CT * g + c + 1)
                    sp.dma_start(mixT_dram[D - CD + c * P:D - CD + (c + 1) * P, bass.ds(g * BANK, BANK)],
                                 y[:, c % 2, :]).then_inc(y_stored[c % 2], DMA)

            groups(sp, body)
            for b in range(2):
                sp.wait_ge(y_stored[b], DMA * GROUPS * CT // 2)

        @block.gpsimd
        def _(pool):
            def x_rstd(t, b):
                pool.wait_ge(ss_done, t + 1)
                nc.gpsimd.tensor_tensor(msq[:, b:b + 1], ss[:, b:b + 1], cst["eps"][:, 0:1],
                                        ALU.add).then_inc(msq_done, 1)
                pool.wait_ge(msq_done, t + 1)
                nc.gpsimd.tensor_tensor(rstd[:, b:b + 1], msq[:, b:b + 1], cst["minus_half"][:, 0:1],
                                        ALU.pow).then_inc(rstd_done, 1)

            with pool.Fori(0, GROUPS) as g:
                for c in range(GT):
                    x_rstd(g * GT + c, c % 2)

        @block.scalar
        def _(act):
            def x_square(g, c):
                t = g * GT + c
                act.wait_ge(x_in[c % 2], g * (DMA * GT // 2) + DMA * (c // 2 + 1))
                wait(act, ss_done, t)
                wait(act, rstd_done, t - 1)
                nc.scalar.activation(square[:, :], x_t[:, c % 2, :], ACT.Square, scale=D ** -0.5,
                                     accum_out=ss[:, c % 2:c % 2 + 1]).then_inc(ss_done, 1)

            for c in range(GT):
                x_square(0, c)
            for k in range(KT):
                act.wait_ge(w_in_sem[k % 2], DMA * (k // 2 + 1))
                nc.scalar.activation(w_hi[:, k, :], w_stage[:, k % 2, :], ACT.Copy).then_inc(w_hi_done, 1)

            def body(g, more):
                for i in range(GT):
                    for n in range(NB):
                        f = i * NB + n
                        act.wait_ge(tx_full, GT * NB * g + f + 1)
                        wait(act, proj_full, 3 * CT * g)
                        nc.scalar.activation(hT_hi[:, 4 * n:4 * n + 4, i * P:(i + 1) * P], tr[:, f % 2, :, :],
                                             ACT.Copy).then_inc(hT_hi_done, 1)
                for c in range(CT):
                    if more:
                        x_square(g + 1, c)
                    act.wait_ge(proj_full, 3 * CT * g + 3 * c + 3)
                    wait(act, y_done, CT * g + c)
                    nc.scalar.activation(u_sb[:, :], proj[:, c % 2, 2, :], ACT.Copy).then_inc(u_done, 1)

            groups(act, body)

        @block.vector
        def _(dve):
            nc.vector.memset(cu[:, :, 0:HALO], 0.0).then_inc(conv_chain, 1)

            def x_norm(g, c):
                t = g * GT + c
                dve.wait_ge(rstd_done, t + 1)
                wait(dve, tx_full, GT * NB * g)
                nc.vector.scalar_tensor_tensor(out=xn[:, c, :], in0=x_t[:, c % 2, :], scalar=rstd[:, c % 2:c % 2 + 1],
                                               in1=gain[:, :], op0=ALU.mult, op1=ALU.mult).then_inc(xn_done, 1)

            dve.wait_ge(gains_in, DMA * (1 + CT))
            for c in range(GT):
                x_norm(0, c)
            for k in range(KT):
                dve.wait_ge(w_hi_done, k + 1)
                nc.vector.tensor_tensor(w_lo[:, k, :], w_stage[:, k % 2, :], w_hi[:, k, :].bitcast(F32),
                                        ALU.subtract).then_inc(w_lo_done, 1)

            CHAIN = TAPS + 2

            def body(g, more):
                for i in range(GT):
                    for n in range(NB):
                        f = i * NB + n
                        dve.wait_ge(hT_hi_done, GT * NB * g + f + 1)
                        nc.vector.tensor_tensor(hT_lo[:, 4 * n:4 * n + 4, i * P:(i + 1) * P], tr[:, f % 2, :, :],
                                                hT_hi[:, 4 * n:4 * n + 4, i * P:(i + 1) * P].bitcast(F32),
                                                ALU.subtract).then_inc(hT_lo_done, 1)
                for c in range(CT):
                    if more:
                        x_norm(g + 1, c)
                    done = g * (CT * CHAIN) + c * CHAIN + 1
                    dve.wait_ge(u_done, CT * g + c + 1)
                    dve.wait_ge(conv_chain, done)
                    nc.vector.tensor_tensor(cu[:, c, HALO:HALO + BANK], proj[:, c % 2, 1, :], u_sb[:, :],
                                            ALU.mult).then_inc(conv_chain, 1)
                    dve.wait_ge(conv_chain, done + 1)
                    wait(dve, y_done, CT * g + c)
                    nc.vector.tensor_scalar(conv[:, :], cu[:, c, HALO:HALO + BANK], taps[:, c, TAPS - 1:TAPS], None,
                                            ALU.mult).then_inc(conv_chain, 1)
                    for w in reversed(range(TAPS - 1)):
                        dve.wait_ge(conv_chain, done + TAPS - w)
                        nc.vector.scalar_tensor_tensor(out=conv[:, :], in0=cu[:, c, w:w + BANK],
                                                       scalar=taps[:, c, w:w + 1], in1=conv[:, :],
                                                       op0=ALU.mult, op1=ALU.add).then_inc(conv_chain, 1)
                    dve.wait_ge(conv_chain, done + TAPS + 1)
                    nc.vector.tensor_copy(cu[:, c, 0:HALO], cu[:, c, BANK:BANK + HALO]).then_inc(conv_chain, 1)
                    wait(dve, y_stored[c % 2], g * (DMA * CT // 2) + DMA * (c // 2))
                    nc.vector.tensor_tensor(y[:, c % 2, :], proj[:, c % 2, 0, :], conv[:, :],
                                            ALU.mult).then_inc(y_done, 1)

            groups(dve, body)

        @block.tensor
        def _(pe):
            pe.wait_ge(w_lo_done, KT)

            def body(g, more):
                for i in range(GT):
                    for n in range(NB):
                        f = i * NB + n
                        pe.wait_ge(xn_done, GT * g + i + 1)
                        if f >= 2:
                            pe.wait_ge(hT_lo_done, GT * NB * g + f - 1)
                        else:
                            wait(pe, hT_lo_done, GT * NB * g)
                        for j in range(4):
                            k = 4 * n + j
                            last = nc.tensor.transpose(tr[:, f % 2, j, :], xn[:, i, k * P:(k + 1) * P],
                                                       cst["ident"][:, :])
                        last.then_inc(tx_full, 1)
                pe.wait_ge(hT_lo_done, GT * NB * (g + 1))
                for c in range(CT):
                    if c >= 2:
                        pe.wait_ge(y_done, CT * g + c - 1)
                    else:
                        wait(pe, y_done, CT * g)
                    for n in (1, 2, 0):
                        col = n * CD + c * P
                        for k in range(KT):
                            last = matmul3(nc, proj[:, c % 2, n, :], w_hi[:, k, col:col + P], w_lo[:, k, col:col + P],
                                           hT_hi[:, k, :], hT_lo[:, k, :], k == 0, k == KT - 1)
                        last.then_inc(proj_full, 1)

            groups(pe, body)


def attend_stage(nc, cst, qk_hi_dram, qk_lo_dram, v_dram, mixT_dram, HD):
    S, AD = v_dram.shape
    HEADS = AD // HD
    KB = S // P
    GT = BANK // P
    NG = 2 * (S // BANK)
    NT = NG * GT
    SLOT = 2 * BANK
    LAG = 2
    SCALE = HD ** -0.5

    def place(n):
        gi, i = n // GT, n % GT
        return gi % 2, GT * (gi // 2) + i, gi

    slots, fills = [0], [0]
    for n in range(NT):
        blocks = place(n)[1] + 1
        slots.append(slots[-1] + -(-blocks * P // SLOT))
        fills.append(fills[-1] + -(-blocks // 4))
    SLOTS, FILLS = slots[-1], fills[-1]
    assert SLOTS % 2 == 0 and FILLS % 4 == 0
    by_vector = [f % 4 == 3 for f in range(FILLS)]
    read_v = [sum(by_vector[:f]) for f in range(FILLS + 1)]
    read_a = [f - read_v[f] for f in range(FILLS + 1)]

    def count(p, per, before):
        return p * per + before

    with ExitStack() as stack:
        m = Pool_(nc, stack, "att_")
        k_st = m.sb("k_st", [P, 2, S], F32R)
        q_hh, q_ll = m.sb("q_hh", [P, 2, S], F32R), m.sb("q_ll", [P, 2, S], F32R)
        v_sb = m.sb("v_sb", [P, 2, KB, HD])
        keep = m.sb("keep", [P, 2, S])
        stick = m.sb("stick", [P, 2, S + 1])
        a = m.sb("a", [P, 4, S])
        aT = m.sb("aT", [P, 2, KB, BANK])
        o_sb = m.sb("o_sb", [HD, 2, BANK])
        z = m.ps("z", [P, 2, SLOT])
        tr = m.ps("tr", [P, 2, 4, P])
        o = m.ps("o", [P, 2, BANK])

        qk_in, v_in = [m.sem("qk_in0"), m.sem("qk_in1")], [m.sem("v_in0"), m.sem("v_in1")]
        z_full, z_read, ones_set = m.sem("z_full"), m.sem("z_read"), m.sem("ones_set")
        scan_done, a_done = m.sem("scan_done"), m.sem("a_done")
        tr_full, aT_by_act, aT_by_dve = m.sem("tr_full"), m.sem("aT_by_act"), m.sem("aT_by_dve")
        o_full, o_read, o_stored = m.sem("o_full"), m.sem("o_read"), [m.sem("o_stored0"), m.sem("o_stored1")]
        QK_LOADS = 6
        block = m.block()

        def at(p, n):
            return (p, n) if n >= 0 else (p - 1, n + NT)

        def pairs(eng, body):
            body(0)
            with eng.Fori(1, HEADS // 2) as p:
                body(p)

        @block.sync
        def _(sp):
            def load_qk(p, h):
                head = 2 * p + h
                rows = bass.ds(head * HD, HD)
                krows = bass.ds(head * HD + AD, HD)
                for half in range(2):
                    part = slice(half * HD, (half + 1) * HD)
                    sp.dma_start(k_st[part, h, :].bitcast(F32), (qk_hi_dram, qk_lo_dram)[half][krows, :]).then_inc(qk_in[h], DMA)
                    sp.dma_start(q_hh[part, h, :].bitcast(F32), qk_hi_dram[rows, :]).then_inc(qk_in[h], DMA)
                    sp.dma_start(q_ll[part, h, :].bitcast(F32), qk_lo_dram[rows, :]).then_inc(qk_in[h], DMA)

            def load_v(p, h):
                cols = bass.ds((2 * p + h) * HD, HD)
                sp.dma_start(v_sb[:, h, :, :],
                             v_dram.rearrange("(j p) d -> p j d", p=P)[:, :, cols]).then_inc(v_in[h], DMA)

            def store(p, gi):
                sp.wait_ge(o_read, count(p, NG, gi + 1))
                h, g = gi % 2, gi // 2
                sp.dma_start(mixT_dram[bass.ds((2 * p + h) * HD, HD), g * BANK:(g + 1) * BANK],
                             o_sb[:, gi % 2, :]).then_inc(o_stored[gi % 2], DMA)

            def body(p):
                for h in range(2):
                    wait(sp, z_full, count(p, SLOTS, slots[NT - GT * (1 - h)] - SLOTS))
                    load_qk(p, h)
                if not isinstance(p, int):
                    store(p - 1, NG - 2)
                    load_v(p, 0)
                    store(p - 1, NG - 1)
                    load_v(p, 1)
                else:
                    load_v(p, 0)
                    load_v(p, 1)
                for gi in range(NG - 2):
                    store(p, gi)

            pairs(sp, body)
            store(HEADS // 2 - 1, NG - 2)
            store(HEADS // 2 - 1, NG - 1)
            for b in range(2):
                sp.wait_ge(o_stored[b], DMA * (NG // 2) * (HEADS // 2))

        def read_fill(eng, copy, p, mt, mine, done):
            p, mt = at(p, mt)
            _, t, gi = place(mt)
            for f in range(fills[mt], fills[mt + 1]):
                if by_vector[f] != mine:
                    continue
                j0 = 4 * (f - fills[mt])
                nj = min(4, t + 1 - j0)
                eng.wait_ge(tr_full, count(p, FILLS, f + 1))
                wait(eng, o_full, count(p, NG, gi - 1))
                copy(aT[:, gi % 2, j0:j0 + nj, (mt % GT) * P:(mt % GT + 1) * P],
                     tr[:, f % 2, 0:nj, :]).then_inc(done, 1)

        @block.scalar
        def _(act):
            def read_o(p, gi):
                act.wait_ge(o_full, count(p, NG, gi + 1))
                wait(act, o_stored[gi % 2], p * (DMA * NG // 2) + DMA * (gi // 2))
                nc.scalar.activation(o_sb[:, gi % 2, :], o[0:HD, gi % 2, :], ACT.Copy).then_inc(o_read, 1)

            def copy(out, in_):
                return nc.scalar.activation(out, in_, ACT.Copy)

            def body(p):
                for n in range(NT):
                    _, t, gi = place(n)
                    L = P * (t + 1)
                    wait(act, scan_done, count(p, NT, n - 1))
                    if n >= 4 or not isinstance(p, int):
                        q, mt = at(p, n - 4)
                        act.wait_ge(tr_full, count(q, FILLS, fills[mt + 1]))
                    for s in range(slots[n], slots[n + 1]):
                        c0 = SLOT * (s - slots[n])
                        c1 = min(L, c0 + SLOT)
                        act.wait_ge(z_full, count(p, SLOTS, s + 1))
                        nc.scalar.activation(keep[:, n % 2, c0:c1], z[:, s % 2, 0:c1 - c0], ACT.Sigmoid,
                                             scale=-SCALE)
                        nc.scalar.activation(a[:, n % 4, c0:c1], z[:, s % 2, 0:c1 - c0], ACT.Sigmoid,
                                             scale=SCALE).then_inc(z_read, 1)
                    if n >= LAG or not isinstance(p, int):
                        read_fill(act, copy, p, n - LAG, False, aT_by_act)
                    mt = n - LAG
                    if mt % GT == 0:
                        gi = mt // GT - 2
                        if gi >= 0:
                            read_o(p, gi)
                        elif not isinstance(p, int):
                            read_o(p - 1, gi + NG)

            pairs(act, body)
            last = HEADS // 2 - 1
            for mt in range(NT - LAG, NT):
                read_fill(act, copy, last, mt, False, aT_by_act)
            read_o(last, NG - 2)
            read_o(last, NG - 1)

        @block.vector
        def _(dve):
            nc.vector.memset(stick[:, :, S:S + 1], 1.0).then_inc(ones_set, 1)
            dve.wait_ge(ones_set, 1)

            def body(p):
                for n in range(NT):
                    _, t, gi = place(n)
                    L = P * (t + 1)
                    if n >= LAG or not isinstance(p, int):
                        read_fill(dve, nc.vector.tensor_copy, p, n - LAG, True, aT_by_dve)
                    dve.wait_ge(z_read, count(p, SLOTS, slots[n + 1]))
                    wait(dve, a_done, count(p, NT, n - 1))
                    right = stick[:, n % 2, S - L:S]
                    nc.vector.tensor_tensor_scan(right[:, ::-1], keep[:, n % 2, 0:L][:, ::-1],
                                                 keep[:, n % 2, 0:L][:, ::-1], 1.0,
                                                 ALU.mult, ALU.bypass).then_inc(scan_done, 1)
                    dve.wait_ge(scan_done, count(p, NT, n + 1))
                    nc.vector.tensor_tensor(a[:, n % 4, 0:L], a[:, n % 4, 0:L], stick[:, n % 2, S - L + 1:S + 1],
                                            ALU.mult).then_inc(a_done, 1)

            pairs(dve, body)
            for mt in range(NT - LAG, NT):
                read_fill(dve, nc.vector.tensor_copy, HEADS // 2 - 1, mt, True, aT_by_dve)

        @block.tensor
        def _(pe):
            def scores(p, n):
                h, t, gi = place(n)
                L = P * (t + 1)
                if n in (0, GT):
                    pe.wait_ge(qk_in[h], (p + 1) * (DMA * QK_LOADS))
                tile = slice(t * P, (t + 1) * P)
                for s in range(slots[n], slots[n + 1]):
                    wait(pe, z_read, count(p, SLOTS, s - 1))
                    c0 = SLOT * (s - slots[n])
                    c1 = min(L, c0 + SLOT)
                    for b0 in range(c0, c1, BANK):
                        b1 = min(c1, b0 + BANK)
                        out = z[:, s % 2, b0 - c0:b1 - c0]
                        nc.tensor.matmul(out, q_hh[:, h, tile], k_st[:, h, b0:b1], start=True, stop=False)
                        last = nc.tensor.matmul(out, q_ll[:, h, tile], k_st[:, h, b0:b1], start=False, stop=b1 < L)
                        if b1 == L:
                            last = nc.tensor.matmul(z[:, s % 2, L - P - c0:L - c0], cst["ident_bf"][:, :],
                                                    cst["mask_bf"][:, :], start=False, stop=True)
                    last.then_inc(z_full, 1)

            def transposes(p, mt):
                p, mt = at(p, mt)
                _, t, gi = place(mt)
                pe.wait_ge(a_done, count(p, NT, mt + 1))
                for f in range(fills[mt], fills[mt + 1]):
                    e = f - 2
                    back = 0 if e >= 0 else FILLS
                    if by_vector[e + back]:
                        wait(pe, aT_by_dve, count(p, read_v[FILLS], read_v[e + back + 1] - (read_v[FILLS] if back else 0)))
                    else:
                        wait(pe, aT_by_act, count(p, read_a[FILLS], read_a[e + back + 1] - (read_a[FILLS] if back else 0)))
                    j0 = 4 * (f - fills[mt])
                    nj = min(4, t + 1 - j0)
                    for j in range(nj):
                        last = nc.tensor.transpose(tr[:, f % 2, j, :], a[:, mt % 4, (j0 + j) * P:(j0 + j + 1) * P],
                                                   cst["ident"][:, :])
                    last.then_inc(tr_full, 1)

            def a_times_v(p, gi, part):
                if gi < 0:
                    p, gi = p - 1, gi + NG
                h, g = gi % 2, gi // 2
                if part == 0:
                    end = fills[(gi + 1) * GT]
                    pe.wait_ge(aT_by_act, count(p, read_a[FILLS], read_a[end]))
                    pe.wait_ge(aT_by_dve, count(p, read_v[FILLS], read_v[end]))
                    pe.wait_ge(v_in[h], (p + 1) * DMA)
                    wait(pe, o_read, count(p, NG, gi - 1))
                for j in range(part * (g + 1), (part + 1) * (g + 1)):
                    c = max(0, j - GT * g) * P
                    last = nc.tensor.matmul(o[0:HD, gi % 2, c:BANK], v_sb[:, h, j, :], aT[:, gi % 2, j, c:BANK],
                                            start=j == 0, stop=j == GT * (g + 1) - 1)
                if part == GT - 1:
                    last.then_inc(o_full, 1)

            def body(p):
                for n in range(NT):
                    scores(p, n)
                    mt = n - LAG
                    if mt >= 0 or not isinstance(p, int):
                        transposes(p, mt)
                        if mt // GT - 1 >= 0 or not isinstance(p, int):
                            a_times_v(p, mt // GT - 1, mt % GT)

            pairs(pe, body)
            last = HEADS // 2 - 1
            for mt in range(NT - LAG, NT):
                transposes(last, mt)
                a_times_v(last, NG - 2, mt % GT)
            for part in range(GT):
                a_times_v(last, NG - 1, part)


def mix_stage(nc, cst, G, acc, h2T_hi, h2T_lo, x, norm_ffn, w_out, mixT_dram):
    S, D = x.shape
    TOK = acc.shape[1] * P
    TILES = TOK // P
    KT = D // P
    NH = D // BANK
    NB = KT // 4
    with ExitStack() as stack:
        m = Pool_(nc, stack, f"mix{G}_")
        w_stage = m.sb("w_stage", [P, 2, D])
        w_hi, w_lo = m.sb("w_hi", [P, KT, D], F32R), m.sb("w_lo", [P, KT, D], F32R)
        mix_t = m.sb("mix_t", [P, 2, KT, P])
        mix_hi, mix_lo = m.sb("mix_hi", [P, 2, KT, P], F32R), m.sb("mix_lo", [P, 2, KT, P], F32R)
        gain = m.sb("gain", [P, D])
        square = m.sb("square", [P, D], BF16)
        ss, msq, rstd = m.sb("ss", [P, 1]), m.sb("msq", [P, 1]), m.sb("rstd", [P, 1])
        xn = m.sb("xn", [P, D])
        proj = m.ps("proj", [P, 2, NH, BANK])
        tr = m.ps("tr", [P, 2, 4, P])

        gain_in, acc_in, mix_in = m.sem("gain_in"), m.sem("acc_in"), [m.sem("mix_in0"), m.sem("mix_in1")]
        w_in_sem = [m.sem("w_in0"), m.sem("w_in1")]
        w_hi_done, w_lo_done, mix_hi_done, mix_lo_done = (
            m.sem(n) for n in ("w_hi_done", "w_lo_done", "mix_hi_done", "mix_lo_done"))
        proj_full, acc_done, ss_done, msq_done, rstd_done, xn_done = (
            m.sem(n) for n in ("proj_full", "acc_done", "ss_done", "msq_done", "rstd_done", "xn_done"))
        tr_full, hT_hi_done, hT_lo_done = m.sem("tr_full"), m.sem("hT_hi_done"), m.sem("hT_lo_done")
        block = m.block()

        def tiles(eng, step):
            step(0, 0, first=True)
            step(1, 1)
            step(2, 0)
            with eng.Fori(1, (TILES - 2) // 2) as i:
                step(2 * i + 1, 1)
                step(2 * i + 2, 0)
            step(TILES - 1, (TILES - 1) % 2, last=True)

        @block.sync
        def _(sp):
            def load(t, b):
                wait(sp, mix_lo_done, t - 1)
                sp.dma_start(mix_t[:, b, :, :], mixT_dram.rearrange("(k p) t -> p k t", p=P)
                             [:, :, bass.ds(G * TOK + t * P, P)]).then_inc(mix_in[b], DMA)

            load(0, 0)
            sp.dma_start(gain[:, :], norm_ffn.partition_broadcast(P)).then_inc(gain_in, DMA)
            for k in range(KT):
                wait(sp, w_lo_done, k - 1)
                sp.dma_start(w_stage[:, k % 2, :], w_out[k * P:(k + 1) * P, :]).then_inc(w_in_sem[k % 2], DMA)
                if k == 1:
                    sp.dma_start(acc[:, :, :], x[G * TOK:(G + 1) * TOK, :].rearrange("(t p) d -> p t d", p=P)
                                 ).then_inc(acc_in, DMA)

            def step(t, b, first=False, last=False):
                if not last:
                    load(t + 1, 1 - b)

            tiles(sp, step)

        @block.gpsimd
        def _(pool):
            with pool.Fori(0, TILES) as t:
                pool.wait_ge(ss_done, t + 1)
                pool.wait_ge(xn_done, t)
                nc.gpsimd.tensor_tensor(msq[:, :], ss[:, :], cst["eps"][:, 0:1], ALU.add).then_inc(msq_done, 1)
                pool.wait_ge(msq_done, t + 1)
                nc.gpsimd.tensor_tensor(rstd[:, :], msq[:, :], cst["minus_half"][:, 0:1],
                                        ALU.pow).then_inc(rstd_done, 1)

        @block.scalar
        def _(act):
            def mix_split(t, b):
                act.wait_ge(mix_in[b], (t - b) * (DMA // 2) + DMA)
                wait(act, proj_full, NH * (t - 1))
                nc.scalar.activation(mix_hi[:, b, :, :], mix_t[:, b, :, :], ACT.Copy).then_inc(mix_hi_done, 1)

            def hT_part(t, n):
                act.wait_ge(tr_full, NB * t + n + 1)
                nc.scalar.activation(h2T_hi[:, 4 * n:4 * n + 4, bass.ds(t * P, P)], tr[:, n % 2, :, :],
                                     ACT.Copy).then_inc(hT_hi_done, 1)

            mix_split(0, 0)
            for k in range(KT):
                act.wait_ge(w_in_sem[k % 2], DMA * (k // 2 + 1))
                nc.scalar.activation(w_hi[:, k, :], w_stage[:, k % 2, :], ACT.Copy).then_inc(w_hi_done, 1)

            def step(t, b, first=False, last=False):
                if not last:
                    mix_split(t + 1, 1 - b)
                if not first:
                    for n in range(NB):
                        hT_part(t - 1, n)
                act.wait_ge(acc_done, NH * (t + 1))
                wait(act, msq_done, t)
                wait(act, ss_done, t)
                nc.scalar.activation(square[:, :], acc[:, t, :], ACT.Square, scale=D ** -0.5,
                                     accum_out=ss[:, :]).then_inc(ss_done, 1)

            tiles(act, step)
            for n in range(NB):
                hT_part(TILES - 1, n)

        @block.vector
        def _(dve):
            def mix_split(t, b):
                dve.wait_ge(mix_hi_done, t + 1)
                nc.vector.tensor_tensor(mix_lo[:, b, :, :], mix_t[:, b, :, :], mix_hi[:, b, :, :].bitcast(F32),
                                        ALU.subtract).then_inc(mix_lo_done, 1)

            def hT_part(t, n):
                dve.wait_ge(hT_hi_done, NB * t + n + 1)
                nc.vector.tensor_tensor(h2T_lo[:, 4 * n:4 * n + 4, bass.ds(t * P, P)], tr[:, n % 2, :, :],
                                        h2T_hi[:, 4 * n:4 * n + 4, bass.ds(t * P, P)].bitcast(F32),
                                        ALU.subtract).then_inc(hT_lo_done, 1)

            mix_split(0, 0)
            for k in range(KT):
                dve.wait_ge(w_hi_done, k + 1)
                nc.vector.tensor_tensor(w_lo[:, k, :], w_stage[:, k % 2, :], w_hi[:, k, :].bitcast(F32),
                                        ALU.subtract).then_inc(w_lo_done, 1)
            dve.wait_ge(acc_in, DMA)
            dve.wait_ge(gain_in, DMA)

            def step(t, b, first=False, last=False):
                if not last:
                    mix_split(t + 1, 1 - b)
                if not first:
                    for n in range(NB):
                        hT_part(t - 1, n)
                for n in range(NH):
                    dve.wait_ge(proj_full, NH * t + n + 1)
                    nc.vector.tensor_tensor(acc[:, t, n * BANK:(n + 1) * BANK], acc[:, t, n * BANK:(n + 1) * BANK],
                                            proj[:, b, n, :], ALU.add).then_inc(acc_done, 1)
                dve.wait_ge(rstd_done, t + 1)
                wait(dve, tr_full, NB * t)
                dve.wait_ge(acc_done, NH * (t + 1))
                nc.vector.scalar_tensor_tensor(out=xn[:, :], in0=acc[:, t, :], scalar=rstd[:, 0:1], in1=gain[:, :],
                                               op0=ALU.mult, op1=ALU.mult).then_inc(xn_done, 1)

            tiles(dve, step)
            for n in range(NB):
                hT_part(TILES - 1, n)

        @block.tensor
        def _(pe):
            pe.wait_ge(w_lo_done, KT)

            def transposes(t):
                pe.wait_ge(xn_done, t + 1)
                for n in range(NB):
                    wait(pe, hT_lo_done, NB * t)
                    for j in range(4):
                        k = 4 * n + j
                        last = nc.tensor.transpose(tr[:, n % 2, j, :], xn[:, k * P:(k + 1) * P], cst["ident"][:, :])
                    last.then_inc(tr_full, 1)

            def step(t, b, first=False, last=False):
                pe.wait_ge(mix_lo_done, t + 1)
                wait(pe, acc_done, NH * (t - 1))
                for n in range(NH):
                    cols = slice(n * BANK, (n + 1) * BANK)
                    for k in range(KT):
                        last_mm = matmul3(nc, proj[:, b, n, :], mix_hi[:, b, k, :], mix_lo[:, b, k, :],
                                          w_hi[:, k, cols], w_lo[:, k, cols], k == 0, k == KT - 1)
                    last_mm.then_inc(proj_full, 1)
                    if n == 0 and not first:
                        transposes(t - 1)

            tiles(pe, step)
            transposes(TILES - 1)


def ffn_stage(nc, cst, G, acc, h2T_hi, h2T_lo, w_gate, w_up, w_down, out):
    D, FF = w_gate.shape
    KT = D // P
    TOK = acc.shape[1] * P
    TILES = TOK // P
    NT = TOK // BANK
    NH = D // BANK
    CHUNKS = FF // P
    PER = TILES // (2 * NT)
    with ExitStack() as stack:
        m = Pool_(nc, stack, f"ffn{G}_")
        gu_stage, d_stage = m.sb("gu_stage", [P, 2, 2, KT, P]), m.sb("d_stage", [P, 2, D])
        gu_hi, gu_lo = m.sb("gu_hi", [P, 2, 2, KT, P], F32R), m.sb("gu_lo", [P, 2, 2, KT, P], F32R)
        d_hi, d_lo = m.sb("d_hi", [P, 2, D], F32R), m.sb("d_lo", [P, 2, D], F32R)
        silu = m.sb("silu", [P, 2, BANK])
        hid = m.sb("hid", [P, 2, BANK])
        hid_hi, hid_lo = m.sb("hid_hi", [P, 2, TOK], F32R), m.sb("hid_lo", [P, 2, TOK], F32R)
        gate, up = m.ps("gate", [P, 2, BANK]), m.ps("up", [P, 2, BANK])
        down = m.ps("down", [P, 2, NH, BANK])

        gu_in, d_in = [m.sem("gu_in0"), m.sem("gu_in1")], [m.sem("d_in0"), m.sem("d_in1")]
        gu_hi_done, gu_lo_done, d_hi_done, d_lo_done = (
            m.sem(n) for n in ("gu_hi_done", "gu_lo_done", "d_hi_done", "d_lo_done"))
        gate_full, up_full, silu_done, hid_done, hid_hi_done, hid_lo_done = (
            m.sem(n) for n in ("gate_full", "up_full", "silu_done", "hid_done", "hid_hi_done", "hid_lo_done"))
        down_full, acc_done, stored = m.sem("down_full"), m.sem("acc_done"), m.sem("stored")
        block = m.block()

        def chunks(eng, step):
            step(0, 0, first=True)
            step(1, 1)
            step(2, 0)
            with eng.Fori(1, (CHUNKS - 2) // 2) as i:
                step(2 * i + 1, 1)
                step(2 * i + 2, 0)
            step(CHUNKS - 1, (CHUNKS - 1) % 2, last=True)

        @block.sync
        def _(sp):
            def load_gu(c, b):
                wait(sp, gu_lo_done, c - 1)
                for j, w in enumerate((w_gate, w_up)):
                    sp.dma_start(gu_stage[:, b, j, :, :], w.rearrange("(k p) f -> p k f", p=P)
                                 [:, :, bass.ds(c * P, P)]).then_inc(gu_in[b], DMA)

            def load_d(c, b):
                wait(sp, d_lo_done, c - 1)
                sp.dma_start(d_stage[:, b, :], w_down[bass.ds(c * P, P), :]).then_inc(d_in[b], DMA)

            load_gu(0, 0)

            def step(c, b, first=False, last=False):
                if not last:
                    load_gu(c + 1, 1 - b)
                load_d(c, b)

            chunks(sp, step)
            for t in range(TILES):
                sp.wait_ge(acc_done, TILES * (CHUNKS - 1) + t + 1)
                sp.dma_start(out[G * TOK + t * P:G * TOK + (t + 1) * P, :], acc[:, t, :]).then_inc(stored, DMA)
            sp.wait_ge(stored, DMA * TILES)

        @block.scalar
        def _(act):
            def gu_split(c, b):
                act.wait_ge(gu_in[b], (c - b) * DMA + 2 * DMA)
                wait(act, up_full, NT * (c - 1))
                nc.scalar.activation(gu_hi[:, b, :, :, :], gu_stage[:, b, :, :, :], ACT.Copy).then_inc(gu_hi_done, 1)

            gu_split(0, 0)

            def step(c, b, first=False, last=False):
                for n in range(NT):
                    act.wait_ge(gate_full, NT * c + n + 1)
                    wait(act, hid_done, NT * (c - 1) + n + 1)
                    nc.scalar.activation(silu[:, n % 2, :], gate[:, n % 2, :], ACT.Silu).then_inc(silu_done, 1)
                    if n == 0 and not last:
                        gu_split(c + 1, 1 - b)
                    if n == 1:
                        act.wait_ge(d_in[b], (c - b) * (DMA // 2) + DMA)
                        wait(act, down_full, TILES * (c - 1))
                        nc.scalar.activation(d_hi[:, b, :], d_stage[:, b, :], ACT.Copy).then_inc(d_hi_done, 1)
                    act.wait_ge(hid_done, NT * c + n + 1)
                    wait(act, down_full, TILES * (c - 1))
                    nc.scalar.activation(hid_hi[:, b, n * BANK:(n + 1) * BANK], hid[:, n % 2, :],
                                         ACT.Copy).then_inc(hid_hi_done, 1)

            chunks(act, step)

        @block.vector
        def _(dve):
            def gu_split(c, b):
                dve.wait_ge(gu_hi_done, c + 1)
                nc.vector.tensor_tensor(gu_lo[:, b, :, :, :], gu_stage[:, b, :, :, :],
                                        gu_hi[:, b, :, :, :].bitcast(F32), ALU.subtract).then_inc(gu_lo_done, 1)

            gu_split(0, 0)

            def add_tiles(c, t0):
                for t in range(t0, t0 + PER):
                    dve.wait_ge(down_full, TILES * c + t + 1)
                    wait(dve, acc_done, TILES * (c - 1) + t + 1)
                    nc.vector.tensor_tensor(acc[:, t, :], acc[:, t, :],
                                            down[:, t % 2, :, :].rearrange("p h n -> p (h n)"),
                                            ALU.add).then_inc(acc_done, 1)

            def step(c, b, first=False, last=False):
                for n in range(NT):
                    if not first:
                        add_tiles(c - 1, 2 * n * PER)
                    dve.wait_ge(silu_done, NT * c + n + 1)
                    dve.wait_ge(up_full, NT * c + n + 1)
                    wait(dve, hid_lo_done, NT * (c - 1) + n + 1)
                    nc.vector.tensor_tensor(hid[:, n % 2, :], silu[:, n % 2, :], up[:, n % 2, :],
                                            ALU.mult).then_inc(hid_done, 1)
                    if n == 0 and not last:
                        gu_split(c + 1, 1 - b)
                    if not first:
                        add_tiles(c - 1, (2 * n + 1) * PER)
                    if n == 1:
                        dve.wait_ge(d_hi_done, c + 1)
                        nc.vector.tensor_tensor(d_lo[:, b, :], d_stage[:, b, :], d_hi[:, b, :].bitcast(F32),
                                                ALU.subtract).then_inc(d_lo_done, 1)
                    dve.wait_ge(hid_hi_done, NT * c + n + 1)
                    nc.vector.tensor_tensor(hid_lo[:, b, n * BANK:(n + 1) * BANK], hid[:, n % 2, :],
                                            hid_hi[:, b, n * BANK:(n + 1) * BANK].bitcast(F32),
                                            ALU.subtract).then_inc(hid_lo_done, 1)

            chunks(dve, step)
            for part in range(2 * NT):
                add_tiles(CHUNKS - 1, part * PER)

        @block.tensor
        def _(pe):
            def hidden(c, b, n, j, bank, full):
                for k in range(KT):
                    toks = slice(n * BANK, (n + 1) * BANK)
                    last = matmul3(nc, bank[:, n % 2, :], gu_hi[:, b, j, k, :], gu_lo[:, b, j, k, :],
                                   h2T_hi[:, k, toks], h2T_lo[:, k, toks], k == 0, k == KT - 1)
                last.then_inc(full, 1)

            def down_tiles(c, b, t0):
                pe.wait_ge(hid_lo_done, NT * (c + 1))
                pe.wait_ge(d_lo_done, c + 1)
                for t in range(t0, t0 + PER):
                    wait(pe, acc_done, TILES * c + t - 1)
                    for h in range(NH):
                        toks, cols = slice(t * P, (t + 1) * P), slice(h * BANK, (h + 1) * BANK)
                        last = matmul3(nc, down[:, t % 2, h, :], hid_hi[:, b, toks], hid_lo[:, b, toks],
                                       d_hi[:, b, cols], d_lo[:, b, cols], True, True)
                    last.then_inc(down_full, 1)

            def step(c, b, first=False, last=False):
                pe.wait_ge(gu_lo_done, c + 1)
                for n in range(NT):
                    wait(pe, silu_done, NT * (c - 1) + n + 1)
                    hidden(c, b, n, 0, gate, gate_full)
                    if not first:
                        down_tiles(c - 1, 1 - b, 2 * n * PER)
                    wait(pe, hid_done, NT * (c - 1) + n + 1)
                    hidden(c, b, n, 1, up, up_full)
                    if not first:
                        down_tiles(c - 1, 1 - b, (2 * n + 1) * PER)

            chunks(pe, step)
            for part in range(2 * NT):
                down_tiles(CHUNKS - 1, (CHUNKS - 1) % 2, part * PER)


def decoder_layer(nc, x, norm_mix, w_in, q_norm, k_norm, conv_w, w_out, norm_ffn, w_gate, w_up, w_down, out):
    x, out = x[0, :, :], out[0, :, :]
    norm_mix, q_norm, k_norm, norm_ffn = norm_mix[0, :], q_norm[0, :], k_norm[0, :], norm_ffn[0, :]
    w_in, conv_w, w_out = w_in[0, :, :], conv_w[0, :, :], w_out[0, :, :]
    w_gate, w_up, w_down = w_gate[0, :, :], w_up[0, :, :], w_down[0, :, :]
    S, D = x.shape
    HD = q_norm.shape[0]
    CD = conv_w.shape[1]
    AD = D - CD
    HALVES = 2
    qk_hi_dram = nc.dram_tensor("qk_hi", [2 * AD, S], F32).ap()
    qk_lo_dram = nc.dram_tensor("qk_lo", [2 * AD, S], F32).ap()
    v_dram = nc.dram_tensor("v_rows", [S, AD], F32).ap()
    mixT_dram = nc.dram_tensor("mixT", [D, S], F32).ap()
    with ExitStack() as stack:
        m = Pool_(nc, stack, "all_")
        cst = {
            "ident": m.sb("ident", [P, P]),
            "ident_bf": m.sb("ident_bf", [P, P], BF16),
            "mask_bf": m.sb("mask_bf", [P, P], BF16),
            "minus_half": m.sb("minus_half", [P, 2 * AD // HD]),
            "eps": m.sb("eps", [P, 2 * AD // HD]),
        }
        constants(nc, cst)
        qkv_stage(nc, cst, x, norm_mix, w_in, q_norm, k_norm, qk_hi_dram, qk_lo_dram, v_dram)
        conv_stage(nc, cst, x, norm_mix, w_in, conv_w, mixT_dram)
        attend_stage(nc, cst, qk_hi_dram, qk_lo_dram, v_dram, mixT_dram, HD)
        acc = m.sb("acc", [P, S // HALVES // P, D])
        h2T_hi = m.sb("h2T_hi", [P, D // P, S // HALVES], F32R)
        h2T_lo = m.sb("h2T_lo", [P, D // P, S // HALVES], F32R)
        for G in range(HALVES):
            mix_stage(nc, cst, G, acc, h2T_hi, h2T_lo, x, norm_ffn, w_out, mixT_dram)
            ffn_stage(nc, cst, G, acc, h2T_hi, h2T_lo, w_gate, w_up, w_down, out)


_INS = ["x", "norm_mix", "w_in", "q_norm", "k_norm", "conv_w", "w_out", "norm_ffn", "w_gate", "w_up", "w_down"]


def kernel(**inputs):
    import numpy as np
    import concourse.bacc as bacc
    from concourse.bass_utils import run_bass_kernel_spmd

    nc = bacc.Bacc("TRN2", target_bir_lowering=False, num_devices=1)
    arrays, args = {}, []
    for name in _INS:
        a = np.ascontiguousarray(inputs[name])
        arrays[f"in_{name}"] = a
        args.append(nc.dram_tensor(f"in_{name}", a.shape, mybir.dt.from_np(a.dtype), kind="ExternalInput").ap())
    out = nc.dram_tensor("out", inputs["x"].shape, F32, kind="ExternalOutput").ap()
    decoder_layer(nc, *args, out)
    r = run_bass_kernel_spmd(nc, [arrays], core_ids=[0])
    return r.results[0]["out"]
```

```python
from contextlib import ExitStack

import concourse.bass as bass
from concourse import mybir

F32 = mybir.dt.float32
F32R = mybir.dt.float32r
BF16 = mybir.dt.bfloat16
ACT = mybir.ActivationFunctionType
ALU = mybir.AluOpType
AX = mybir.AxisListType

P = 128
BANK = 512
EPS = 1e-6
MASKED = -1e30
DMA = 16


def wait(eng, sem, value):
    if not isinstance(value, int) or value > 0:
        eng.wait_ge(sem, value)


class Pool_:

    def __init__(self, nc, stack, prefix):
        self.nc, self.stack, self.prefix = nc, stack, prefix

    def sb(self, name, shape, dt=F32):
        return self.stack.enter_context(self.nc.sbuf_tensor(self.prefix + name, shape, dt))

    def ps(self, name, shape, dt=F32):
        return self.stack.enter_context(self.nc.psum_tensor(self.prefix + name, shape, dt))

    def sem(self, name):
        return self.stack.enter_context(self.nc.semaphore(self.prefix + name))

    def block(self):
        return self.stack.enter_context(self.nc.Block())


def matmul3(nc, out, lhs_hi, lhs_lo, rhs_hi, rhs_lo, first, last):
    nc.tensor.matmul(out, lhs_hi, rhs_hi, start=first, stop=False)
    nc.tensor.matmul(out, lhs_hi, rhs_lo, start=False, stop=False)
    return nc.tensor.matmul(out, lhs_lo, rhs_hi, start=False, stop=last)


def constants(nc, cst):
    with ExitStack() as stack:
        m = Pool_(nc, stack, "cst_")
        filled, picked, copied = m.sem("filled"), m.sem("picked"), m.sem("copied")
        mask32 = m.sb("mask32", [P, P])
        block = m.block()

        @block.gpsimd
        def _(pool):
            nc.gpsimd.memset(cst["ident"][:, :], 0.0).then_inc(filled, 1)
            nc.gpsimd.memset(mask32[:, :], 0.0).then_inc(filled, 1)
            nc.gpsimd.memset(cst["minus_half"][:, :], -0.5).then_inc(filled, 1)
            nc.gpsimd.memset(cst["eps"][:, :], EPS).then_inc(filled, 1)
            pool.wait_ge(filled, 4)
            nc.gpsimd.affine_select(out=cst["ident"][:, :], in_=cst["ident"][:, :], compare_op=ALU.not_equal,
                                    fill=1.0, base=0, pattern=[[-1, P]], channel_multiplier=1).then_inc(picked, 1)
            nc.gpsimd.affine_select(out=mask32[:, :], in_=mask32[:, :], compare_op=ALU.is_gt,
                                    fill=MASKED, base=0, pattern=[[-1, P]], channel_multiplier=1).then_inc(picked, 1)

        @block.vector
        def _(dve):
            dve.wait_ge(picked, 2)
            nc.vector.tensor_copy(cst["ident_bf"][:, :], cst["ident"][:, :]).then_inc(copied, 1)
            nc.vector.tensor_copy(cst["mask_bf"][:, :], mask32[:, :]).then_inc(copied, 1)
            dve.wait_ge(copied, 2)


def qkv_stage(nc, cst, x, norm_mix, w_in, q_norm, k_norm, hT_hi_dram, hT_lo_dram, qk_hi_dram, qk_lo_dram, v_dram):
    S, D = x.shape
    KT = D // P
    TILES = S // P
    HD = q_norm.shape[0]
    HEADS = v_dram.shape[1]
    AD = HEADS * HD
    PAIRS = AD // P
    COLS = 3 * AD
    NB = KT // 4
    with ExitStack() as stack:
        m = Pool_(nc, stack, "qkv_")
        w_stage = m.sb("w_stage", [P, 2, COLS])
        w_hi, w_lo = m.sb("w_hi", [P, KT, COLS], F32R), m.sb("w_lo", [P, KT, COLS], F32R)
        gain = m.sb("gain", [P, D])
        qk_gain = m.sb("qk_gain", [P, 2])
        x_t = m.sb("x_t", [P, 2, D])
        square = m.sb("square", [P, D])
        ss, msq, rstd = m.sb("ss", [P, 2]), m.sb("msq", [P, 2]), m.sb("rstd", [P, 2])
        xn = m.sb("xn", [P, 2, D])
        hT_hi, hT_lo = m.sb("hT_hi", [P, 2, KT, P], F32R), m.sb("hT_lo", [P, 2, KT, P], F32R)
        qk_square = m.sb("qk_square", [P, 2 * AD])
        qk_ss, qk_msq, qk_rstd = (m.sb(n, [P, 2 * HEADS]) for n in ("qk_ss", "qk_msq", "qk_rstd"))
        qk_n = m.sb("qk_n", [P, 2 * AD])
        v_out = m.sb("v_out", [P, 2, HEADS, 2 * HD], F32R)
        qkT_hi, qkT_lo = m.sb("qkT_hi", [P, 2, 2 * PAIRS, P], F32R), m.sb("qkT_lo", [P, 2, 2 * PAIRS, P], F32R)
        proj = m.ps("proj", [P, 2, 3, BANK])
        tr_x, tr_qk = m.ps("tr_x", [P, 4, P]), m.ps("tr_qk", [P, 4, P])

        gains_in, x_in = m.sem("gains_in"), [m.sem("x_in0"), m.sem("x_in1")]
        w_in_sem = [m.sem("w_in0"), m.sem("w_in1")]
        w_hi_done, w_lo_done = m.sem("w_hi_done"), m.sem("w_lo_done")
        ss_done, msq_done, rstd_done, xn_done = (m.sem(n) for n in ("ss_done", "msq_done", "rstd_done", "xn_done"))
        tx_full, hT_hi_done, hT_lo_done = m.sem("tx_full"), m.sem("hT_hi_done"), m.sem("hT_lo_done")
        proj_full, square_done = m.sem("proj_full"), m.sem("square_done")
        v_hi_done, v_done = m.sem("v_hi_done"), m.sem("v_done")
        qk_ss_done, qk_msq_done, qk_rstd_done, qk_n_done = (
            m.sem(n) for n in ("qk_ss_done", "qk_msq_done", "qk_rstd_done", "qk_n_done"))
        tq_full, qkT_hi_done, qkT_lo_done = m.sem("tq_full"), m.sem("qkT_hi_done"), m.sem("qkT_lo_done")
        hT_stored = [m.sem("hT_stored0"), m.sem("hT_stored1")]
        v_stored, qkT_stored = [m.sem("v_stored0"), m.sem("v_stored1")], [m.sem("qkT_stored0"), m.sem("qkT_stored1")]
        block = m.block()

        def tiles(eng, step, tail=1):
            step(0, 0, first=True)
            step(1, 1)
            step(2, 0)
            with eng.Fori(1, (TILES - 1 - tail) // 2) as i:
                step(2 * i + 1, 1)
                step(2 * i + 2, 0)
            for t in range(TILES - tail, TILES):
                step(t, t % 2, last=t == TILES - 1)

        @block.sync
        def _(sp):
            for b in range(2):
                sp.dma_start(x_t[:, b, :], x[b * P:(b + 1) * P, :]).then_inc(x_in[b], DMA)
            sp.dma_start(gain[:, :], norm_mix.partition_broadcast(P)).then_inc(gains_in, DMA)
            for j, g in enumerate((q_norm, k_norm)):
                for half in range(P // HD):
                    sp.dma_start(qk_gain[half * HD:(half + 1) * HD, j:j + 1],
                                 g.rearrange("(p o) -> p o", o=1)).then_inc(gains_in, DMA)
            for k in range(KT):
                wait(sp, w_lo_done, k - 1)
                sp.dma_start(w_stage[:, k % 2, :], w_in[k * P:(k + 1) * P, 0:COLS]).then_inc(w_in_sem[k % 2], DMA)

            def step(t, b, first=False, last=False):
                if not isinstance(t, int) or t + 2 < TILES:
                    sp.wait_ge(xn_done, t + 1)
                    sp.dma_start(x_t[:, b, :], x[bass.ds((t + 2) * P, P), :]).then_inc(x_in[b], DMA)
                sp.wait_ge(hT_lo_done, NB * t + NB)
                for src, dst in ((hT_hi, hT_hi_dram), (hT_lo, hT_lo_dram)):
                    sp.dma_start(dst.rearrange("(c p) t -> p c t", p=P)[:, :, bass.ds(t * P, P)],
                                 src[:, b, :, :].bitcast(F32)).then_inc(hT_stored[b], DMA)
                if not first:
                    sp.wait_ge(qkT_lo_done, 2 * t)
                    store_qk(t - 1, 1 - b)
                sp.wait_ge(v_done, t + 1)
                sp.dma_start(v_dram[bass.ds(t * P, P), :, :], v_out[:, b, :, :].bitcast(F32)).then_inc(v_stored[b], DMA)

            def store_qk(t, b):
                for src, dst in ((qkT_hi, qk_hi_dram), (qkT_lo, qk_lo_dram)):
                    sp.dma_start(dst.rearrange("(c p) t -> p c t", p=P)[:, :, bass.ds(t * P, P)],
                                 src[:, b, :, :].bitcast(F32)).then_inc(qkT_stored[b], DMA)

            tiles(sp, step, tail=3)
            sp.wait_ge(qkT_lo_done, 2 * TILES)
            store_qk(TILES - 1, (TILES - 1) % 2)
            for b in range(2):
                sp.wait_ge(v_stored[b], DMA * TILES // 2)
                sp.wait_ge(hT_stored[b], DMA * TILES)
                sp.wait_ge(qkT_stored[b], DMA * TILES)

        @block.gpsimd
        def _(pool):
            def x_rstd(t, b):
                pool.wait_ge(ss_done, t + 1)
                nc.gpsimd.tensor_tensor(msq[:, b:b + 1], ss[:, b:b + 1], cst["eps"][:, 0:1],
                                        ALU.add).then_inc(msq_done, 1)
                pool.wait_ge(msq_done, t + 1)
                nc.gpsimd.tensor_tensor(rstd[:, b:b + 1], msq[:, b:b + 1], cst["minus_half"][:, 0:1],
                                        ALU.pow).then_inc(rstd_done, 1)

            x_rstd(0, 0)

            def step(t, b, first=False, last=False):
                if not last:
                    x_rstd(t + 1, 1 - b)
                pool.wait_ge(qk_ss_done, t + 1)
                nc.gpsimd.tensor_tensor(qk_msq[:, :], qk_ss[:, :], cst["eps"][:, 0:2 * HEADS],
                                        ALU.add).then_inc(qk_msq_done, 1)
                pool.wait_ge(qk_msq_done, t + 1)
                nc.gpsimd.tensor_tensor(qk_rstd[:, :], qk_msq[:, :], cst["minus_half"][:, 0:2 * HEADS],
                                        ALU.pow).then_inc(qk_rstd_done, 1)

            tiles(pool, step)

        @block.scalar
        def _(act):
            def x_square(t, b):
                act.wait_ge(x_in[b], DMA * (t // 2 + 1) if isinstance(t, int) else x_count(t, b))
                wait(act, ss_done, t)
                nc.scalar.activation(square[:, :], x_t[:, b, :], ACT.Square, scale=D ** -0.5,
                                     accum_out=ss[:, b:b + 1]).then_inc(ss_done, 1)

            def x_count(t, b):
                return (t - b) * (DMA // 2) + DMA

            def hT_part(t, b, n):
                act.wait_ge(tx_full, NB * t + n + 1)
                wait(act, proj_full, 3 * (t - 1))
                wait(act, hT_stored[b], DMA * (t - b))
                nc.scalar.activation(hT_hi[:, b, 4 * n:4 * n + 4, :], tr_x[:, :, :], ACT.Copy).then_inc(hT_hi_done, 1)

            def qkT_part(t, b, n):
                act.wait_ge(tq_full, 2 * t + n + 1)
                wait(act, qkT_stored[b], DMA * (t - b))
                nc.scalar.activation(qkT_hi[:, b, PAIRS * n:PAIRS * (n + 1), :], tr_qk[:, :, :], ACT.Copy,
                                     scale=qk_gain[:, n:n + 1]).then_inc(qkT_hi_done, 1)

            def head_square(t, b, n):
                act.wait_ge(proj_full, 3 * t + n + 1)
                wait(act, qk_ss_done, t)
                nc.scalar.activation(qk_square[:, n * AD:(n + 1) * AD], proj[:, b, n, 0:AD],
                                     ACT.Square, scale=HD ** -0.5).then_inc(square_done, 1)

            x_square(0, 0)
            for k in range(KT):
                act.wait_ge(w_in_sem[k % 2], DMA * (k // 2 + 1))
                nc.scalar.activation(w_hi[:, k, :], w_stage[:, k % 2, :], ACT.Copy).then_inc(w_hi_done, 1)
            act.wait_ge(gains_in, DMA * 5)
            for n in range(NB):
                hT_part(0, 0, n)

            def step(t, b, first=False, last=False):
                if not last:
                    x_square(t + 1, 1 - b)
                head_square(t, b, 0)
                if not first:
                    qkT_part(t - 1, 1 - b, 0)
                if not last:
                    hT_part(t + 1, 1 - b, 0)
                head_square(t, b, 1)
                if not first:
                    qkT_part(t - 1, 1 - b, 1)
                if not last:
                    hT_part(t + 1, 1 - b, 1)
                act.wait_ge(proj_full, 3 * t + 3)
                wait(act, v_stored[b], (DMA // 2) * (t - b))
                nc.scalar.activation(v_out[:, b, :, 0:HD], proj[:, b, 2, 0:AD].rearrange("p (h d) -> p h d", d=HD),
                                     ACT.Copy).then_inc(v_hi_done, 1)

            tiles(act, step)
            for n in range(2):
                qkT_part(TILES - 1, (TILES - 1) % 2, n)

        @block.vector
        def _(dve):
            def x_norm(t, b):
                dve.wait_ge(rstd_done, t + 1)
                wait(dve, tx_full, NB * (t - 1))
                nc.vector.scalar_tensor_tensor(out=xn[:, b, :], in0=x_t[:, b, :], scalar=rstd[:, b:b + 1],
                                               in1=gain[:, :], op0=ALU.mult, op1=ALU.mult).then_inc(xn_done, 1)

            def hT_part(t, b, n):
                dve.wait_ge(hT_hi_done, NB * t + n + 1)
                nc.vector.tensor_tensor(hT_lo[:, b, 4 * n:4 * n + 4, :], tr_x[:, :, :],
                                        hT_hi[:, b, 4 * n:4 * n + 4, :].bitcast(F32),
                                        ALU.subtract).then_inc(hT_lo_done, 1)

            def qkT_part(t, b, n):
                dve.wait_ge(qkT_hi_done, 2 * t + n + 1)
                nc.vector.scalar_tensor_tensor(out=qkT_lo[:, b, PAIRS * n:PAIRS * (n + 1), :], in0=tr_qk[:, :, :],
                                               scalar=qk_gain[:, n:n + 1],
                                               in1=qkT_hi[:, b, PAIRS * n:PAIRS * (n + 1), :].bitcast(F32),
                                               op0=ALU.mult, op1=ALU.subtract).then_inc(qkT_lo_done, 1)

            dve.wait_ge(gains_in, DMA * 5)
            x_norm(0, 0)
            for k in range(KT):
                dve.wait_ge(w_hi_done, k + 1)
                nc.vector.tensor_tensor(w_lo[:, k, :], w_stage[:, k % 2, :], w_hi[:, k, :].bitcast(F32),
                                        ALU.subtract).then_inc(w_lo_done, 1)
            for n in range(NB):
                hT_part(0, 0, n)

            def step(t, b, first=False, last=False):
                if not last:
                    x_norm(t + 1, 1 - b)
                if not first:
                    qkT_part(t - 1, 1 - b, 0)
                if not last:
                    hT_part(t + 1, 1 - b, 0)
                dve.wait_ge(square_done, 2 * t + 2)
                wait(dve, qk_rstd_done, t)
                nc.vector.reduce_sum(qk_ss[:, :], qk_square[:, :].rearrange("p (h d) -> p h d", d=HD),
                                     axis=AX.X).then_inc(qk_ss_done, 1)
                if not first:
                    qkT_part(t - 1, 1 - b, 1)
                if not last:
                    hT_part(t + 1, 1 - b, 1)
                dve.wait_ge(qk_rstd_done, t + 1)
                wait(dve, tq_full, 2 * t)
                for n in range(2):
                    nc.vector.tensor_tensor(
                        qk_n[:, n * AD:(n + 1) * AD].rearrange("p (h d) -> p h d", d=HD),
                        proj[:, b, n, 0:AD].rearrange("p (h d) -> p h d", d=HD),
                        qk_rstd[:, n * HEADS:(n + 1) * HEADS].unsqueeze(2).to_broadcast([P, HEADS, HD]),
                        ALU.mult).then_inc(qk_n_done, 1)
                dve.wait_ge(v_hi_done, t + 1)
                nc.vector.tensor_tensor(v_out[:, b, :, HD:2 * HD], proj[:, b, 2, 0:AD].rearrange("p (h d) -> p h d", d=HD),
                                        v_out[:, b, :, 0:HD].bitcast(F32), ALU.subtract).then_inc(v_done, 1)

            tiles(dve, step)
            for n in range(2):
                qkT_part(TILES - 1, (TILES - 1) % 2, n)

        @block.tensor
        def _(pe):
            def x_transpose(t, b, n):
                pe.wait_ge(xn_done, t + 1)
                wait(pe, hT_lo_done, NB * t + n)
                for j in range(4):
                    k = 4 * n + j
                    last = nc.tensor.transpose(tr_x[:, j, :], xn[:, b, k * P:(k + 1) * P], cst["ident"][:, :])
                last.then_inc(tx_full, 1)

            def qk_transpose(t, b, n):
                pe.wait_ge(qk_n_done, 2 * t + n + 1)
                wait(pe, qkT_lo_done, 2 * t + n)
                for j in range(PAIRS):
                    c = n * AD + j * P
                    last = nc.tensor.transpose(tr_qk[:, j, :], qk_n[:, c:c + P], cst["ident"][:, :])
                last.then_inc(tq_full, 1)

            def project(t, b, n):
                if n < 2:
                    wait(pe, qk_n_done, 2 * (t - 1))
                else:
                    wait(pe, v_done, t - 1)
                pe.wait_ge(hT_lo_done, NB * t + NB)
                for k in range(KT):
                    last = matmul3(nc, proj[:, b, n, 0:AD], hT_hi[:, b, k, :], hT_lo[:, b, k, :],
                                   w_hi[:, k, n * AD:(n + 1) * AD], w_lo[:, k, n * AD:(n + 1) * AD],
                                   k == 0, k == KT - 1)
                last.then_inc(proj_full, 1)

            for n in range(NB):
                x_transpose(0, 0, n)
            pe.wait_ge(w_lo_done, KT)

            def step(t, b, first=False, last=False):
                project(t, b, 0)
                if not first:
                    qk_transpose(t - 1, 1 - b, 0)
                if not last:
                    x_transpose(t + 1, 1 - b, 0)
                project(t, b, 1)
                if not first:
                    qk_transpose(t - 1, 1 - b, 1)
                if not last:
                    x_transpose(t + 1, 1 - b, 1)
                project(t, b, 2)

            tiles(pe, step)
            for n in range(2):
                qk_transpose(TILES - 1, (TILES - 1) % 2, n)


def attend_conv_stage(nc, cst, hT_hi_dram, hT_lo_dram, w_in, conv_w, qk_hi_dram, qk_lo_dram, v_dram, mixT_dram, HD):
    D, S = hT_hi_dram.shape
    HEADS = v_dram.shape[1]
    AD = HEADS * HD
    TAPS, CD = conv_w.shape
    KT = D // P
    KB = S // P
    GW = 2 * P
    GT = GW // P
    NG = 2 * (S // GW)
    SLOT = 2 * BANK
    SB = SLOT // P
    LAG = 3
    SCALE = HD ** -0.5
    PAIRS = HEADS // 2
    CT = CD // P
    NPROJ = 3 * CT
    HALO = TAPS - 1
    COL0 = w_in.shape[1] - 3 * CD
    assert S // BANK == PAIRS

    units, opens = [], []
    for gi in range(NG):
        for i in range(GT):
            t = GT * (gi // 2) + i
            for j0 in reversed(range(0, t + 1, SB)):
                opens.append(not units or units[-1][0] != gi)
                units.append((gi, gi % 2, t, j0, min(SB, t + 1 - j0)))
    NU = len(units)
    fills = [0]
    for u in units:
        fills.append(fills[-1] + -(-u[4] // 4))
    FILLS = fills[-1]
    assert NU % 4 == 0 and FILLS % 2 == 0
    group_units = [sum(u[0] < gi for u in units) for gi in range(NG + 1)]
    head_end = [max(n for n, u in enumerate(units) if u[1] == h) + 1 for h in range(2)]
    FIRST, LAST = LAG + 1, NU - 4
    own = [u[4] + (GT * (units[n - LAG][0] // 2 + 1) if n > LAG and opens[n - LAG] else 0)
           for n, u in enumerate(units)]
    weight = [u[4] + 2 for u in units]
    ratio = (sum(own[FIRST:LAST]) + 3 * NPROJ * KT) / sum(weight[FIRST:LAST])
    steps, placed, goal, spent = [[] for _ in units], 0, 0.0, 0.0
    for n in range(FIRST, LAST):
        goal += weight[n] * ratio
        spent += own[n]
        while placed < NPROJ * KT and spent + 1.5 < goal:
            if placed % KT == 0 and steps[n]:
                break
            steps[n].append((placed // KT, placed % KT))
            spent += 3
            placed += 1
    starts = {n: k for n in range(NU) for k, i in steps[n] if i == 0}
    ends = {n: k for n in range(NU) for k, i in steps[n] if i == KT - 1}
    assert len(starts) == len(ends) == NPROJ

    def at(p, n, per=NU):
        return (p, n) if n >= 0 else (p - 1, n + per)

    with ExitStack() as stack:
        m = Pool_(nc, stack, "att_")
        k_st = m.sb("k_st", [P, 2, S], F32R)
        q_hh, q_ll = m.sb("q_hh", [P, 2, 2, GW], F32R), m.sb("q_ll", [P, 2, 2, GW], F32R)
        v_st = m.sb("v_st", [P, 2, KB, 2 * HD], F32R)
        keep = m.sb("keep", [P, 2, SLOT])
        stick = m.sb("stick", [P, 2, SLOT + 1])
        ones = m.sb("ones", [P, 1])
        a = m.sb("a", [P, 4, SLOT])
        aT_hi, aT_lo = m.sb("aT_hi", [P, 2, KB, GW], F32R), m.sb("aT_lo", [P, 2, KB, GW], F32R)
        o_low = m.sb("o_low", [HD, GW])
        o_sb = m.sb("o_sb", [HD, 2, GW])
        hT_hi, hT_lo = m.sb("hT_hi", [P, KT, BANK], F32R), m.sb("hT_lo", [P, KT, BANK], F32R)
        w_stage = m.sb("w_stage", [P, KT, P])
        w_hi, w_lo = m.sb("w_hi", [P, 2, KT, P], F32R), m.sb("w_lo", [P, 2, KT, P], F32R)
        taps = m.sb("taps", [P, CT, TAPS])
        halo = m.sb("halo", [P, CT, HALO])
        c_sb = m.sb("c_sb", [P, BANK])
        cu = m.sb("cu", [P, HALO + BANK])
        conv = m.sb("conv", [P, BANK])
        y = m.sb("y", [P, BANK])
        z = m.ps("z", [P, 2, SLOT])
        tr = m.ps("tr", [P, 2, 4, P])
        o = m.ps("o", [P, BANK])
        proj = m.ps("proj", [P, BANK])

        k_in, v_in = [m.sem("k_in0"), m.sem("k_in1")], [m.sem("v_in0"), m.sem("v_in1")]
        q_in = [[m.sem(f"q_in{h}{b}") for b in range(2)] for h in range(2)]
        hT_in = [m.sem(f"hT_in{i}") for i in range(KT)]
        w_in_sem, taps_in, hT_used = m.sem("w_in"), m.sem("taps_in"), m.sem("hT_used")
        z_full, keep_done, z_read, ones_set = m.sem("z_full"), m.sem("keep_done"), m.sem("z_read"), m.sem("ones_set")
        edge_set, scan_done = m.sem("edge_set"), m.sem("scan_done")
        a_done = [m.sem("a_done0"), m.sem("a_done1")]
        tr_full, aT_hi_done, aT_lo_done = m.sem("tr_full"), m.sem("aT_hi_done"), m.sem("aT_lo_done")
        o_full, o_low_done, o_done = m.sem("o_full"), m.sem("o_low_done"), m.sem("o_done")
        o_stored = [m.sem("o_stored0"), m.sem("o_stored1")]
        w_hi_done, w_lo_done, proj_full = m.sem("w_hi_done"), m.sem("w_lo_done"), m.sem("proj_full")
        c_done, cu_done, conv_chain, y_done, y_stored = (
            m.sem(n) for n in ("c_done", "cu_done", "conv_chain", "y_done", "y_stored"))
        block = m.block()

        def pairs(eng, body):
            body(0)
            with eng.Fori(1, PAIRS) as p:
                body(p)

        @block.sync
        def _(sp):
            def load_k(p, h):
                wait(sp, z_full, NU * p + head_end[h] - NU)
                rows = bass.ds((2 * p + h) * HD + AD, HD)
                for half, src in enumerate((qk_hi_dram, qk_lo_dram)):
                    sp.dma_start(k_st[half * HD:(half + 1) * HD, h, :].bitcast(F32),
                                 src[rows, :]).then_inc(k_in[h], DMA)

            def load_q(p, gi):
                h, g = gi % 2, gi // 2
                q, gq = at(p, gi - 4, NG)
                wait(sp, z_full, q * NU + group_units[gq + 1])
                rows = bass.ds((2 * p + h) * HD, HD)
                for half in range(2):
                    part = slice(half * HD, (half + 1) * HD)
                    for dst, src in ((q_hh, qk_hi_dram), (q_ll, qk_lo_dram)):
                        sp.dma_start(dst[part, h, g % 2, :].bitcast(F32),
                                     src[rows, g * GW:(g + 1) * GW]).then_inc(q_in[h][g % 2], DMA)

            def load_v(p, h):
                wait(sp, o_full, NG * p + h - 1)
                sp.dma_start(v_st[:, h, :, :].bitcast(F32), v_dram.rearrange("(j p) h d -> p j h d", p=P)
                             [:, :, bass.ds(2 * p + h, 1), :].rearrange("p j h d -> p j (h d)")).then_inc(v_in[h], DMA)

            def load_hT(p, i):
                if i < KT - 1:
                    wait(sp, hT_used, (KT - 1) * p - KT + i + 2)
                else:
                    wait(sp, proj_full, NPROJ * p)
                for dst, src in ((hT_hi, hT_hi_dram), (hT_lo, hT_lo_dram)):
                    sp.dma_start(dst[:, i, :].bitcast(F32),
                                 src[i * P:(i + 1) * P, bass.ds(p * BANK, BANK)]).then_inc(hT_in[i], DMA)

            def load_w(p, k):
                wait(sp, w_lo_done, NPROJ * p + k)
                col = COL0 + (1, 2, 0)[k % 3] * CD + (k // 3) * P
                sp.dma_start(w_stage[:, :, :], w_in.rearrange("(k p) f -> p k f", p=P)
                             [:, :, col:col + P]).then_inc(w_in_sem, DMA)

            def store_o(p, gi):
                p, gi = at(p, gi, NG)
                h, g = gi % 2, gi // 2
                sp.wait_ge(o_done, NG * p + gi + 1)
                sp.dma_start(mixT_dram[bass.ds((2 * p + h) * HD, HD), g * GW:(g + 1) * GW],
                             o_sb[:, gi % 2, :]).then_inc(o_stored[gi % 2], DMA)

            with nc.allow_non_contiguous_dma(reason="conv weights, once"):
                for c in range(CT):
                    sp.dma_start(taps[:, c, :], conv_w[:, c * P:(c + 1) * P].rearrange("w p -> p w")
                                 ).then_inc(taps_in, DMA)

            def body(p):
                for n, (gi, h, t, j0, nb) in enumerate(units):
                    if n == 0:
                        load_q(p, 0)
                        load_w(p, 0)
                        load_k(p, 0)
                        for i in range(KT // 2):
                            load_hT(p, i)
                        load_q(p, 1)
                        load_k(p, 1)
                        load_v(p, 0)
                        for i in range(KT // 2, KT):
                            load_hT(p, i)
                    if n == LAG + 1:
                        load_v(p, 1)
                    if opens[n] and gi + 2 < NG:
                        load_q(p, gi + 2)
                    if opens[n] and (gi >= 3 or not isinstance(p, int)):
                        store_o(p, gi - 3)
                    if n == LAG:
                        load_w(p, 1)
                    if n in starts and starts[n] + 2 < NPROJ:
                        load_w(p, starts[n] + 2)
                    if ends.get(n - 2, 0) % 3 == 2:
                        store_y(p, ends[n - 2] // 3)

            def store_y(p, c):
                sp.wait_ge(y_done, CT * p + c + 1)
                row = AD + c * P
                sp.dma_start(mixT_dram[row:row + P, bass.ds(p * BANK, BANK)], y[:, :]).then_inc(y_stored, DMA)

            pairs(sp, body)
            for gi in range(NG - 3, NG):
                store_o(PAIRS - 1, gi)
            for b in range(2):
                sp.wait_ge(o_stored[b], DMA * PAIRS * NG // 2)
            sp.wait_ge(y_stored, DMA * PAIRS * CT)

        @block.scalar
        def _(act):
            def sigmoids(p, n):
                gi, h, t, j0, nb = units[n]
                wait(act, scan_done, NU * p + n - 1)
                q, n4 = at(p, n - 4)
                wait(act, tr_full, FILLS * q + fills[n4 + 1])
                act.wait_ge(z_full, NU * p + n + 1)
                nc.scalar.activation(keep[:, n % 2, 0:nb * P], z[:, n % 2, 0:nb * P], ACT.Sigmoid,
                                     scale=-SCALE).then_inc(keep_done, 1)
                nc.scalar.activation(a[:, n % 4, 0:nb * P], z[:, n % 2, 0:nb * P], ACT.Sigmoid,
                                     scale=SCALE).then_inc(z_read, 1)

            def aT_part(p, n):
                p, n = at(p, n)
                gi, h, t, j0, nb = units[n]
                for f in range(fills[n], fills[n + 1]):
                    j = 4 * (f - fills[n])
                    nj = min(4, nb - j)
                    act.wait_ge(tr_full, FILLS * p + f + 1)
                    wait(act, o_full, NG * p + gi - 1)
                    nc.scalar.activation(aT_hi[:, gi % 2, j0 + j:j0 + j + nj, (t % GT) * P:(t % GT + 1) * P],
                                         tr[:, f % 2, 0:nj, :], ACT.Copy).then_inc(aT_hi_done, 1)

            def o_part(p, gi):
                p, gi = at(p, gi, NG)
                act.wait_ge(o_full, NG * p + gi + 1)
                wait(act, o_done, NG * p + gi)
                nc.scalar.activation(o_low[:, :], o[HD:2 * HD, 0:GW], ACT.Copy).then_inc(o_low_done, 1)

            def w_split(p, k):
                act.wait_ge(w_in_sem, DMA * NPROJ * p + DMA * (k + 1))
                wait(act, proj_full, NPROJ * p + k - 1)
                nc.scalar.activation(w_hi[:, k % 2, :, :], w_stage[:, :, :], ACT.Copy).then_inc(w_hi_done, 1)

            def body(p):
                for n in range(NU):
                    sigmoids(p, n)
                    if ends.get(n - 1, 1) % 3 == 0:
                        c = ends[n - 1] // 3
                        act.wait_ge(proj_full, NPROJ * p + ends[n - 1] + 1)
                        wait(act, cu_done, CT * p + c)
                        nc.scalar.activation(c_sb[:, :], proj[:, :], ACT.Copy).then_inc(c_done, 1)
                    if n >= LAG or not isinstance(p, int):
                        aT_part(p, n - LAG)
                    q, b = at(p, n - LAG - 1)
                    if opens[b] and (n - LAG - 1 > 0 or not isinstance(p, int)):
                        o_part(q, units[b][0] - 1)
                    if n == 1:
                        w_split(p, 0)
                    if n in starts and starts[n] + 1 < NPROJ:
                        w_split(p, starts[n] + 1)

            pairs(act, body)
            for n in range(NU - LAG, NU):
                aT_part(PAIRS - 1, n)
                if opens[n - 1]:
                    o_part(PAIRS - 1, units[n - 1][0] - 1)
            assert not opens[NU - 1]
            o_part(PAIRS - 1, NG - 1)

        @block.vector
        def _(dve):
            nc.vector.memset(ones[:, :], 1.0).then_inc(ones_set, 1)
            nc.vector.memset(halo[:, :, :], 0.0).then_inc(ones_set, 1)
            dve.wait_ge(ones_set, 2)
            dve.wait_ge(taps_in, DMA * CT)

            def running_product(p, n):
                gi, h, t, j0, nb = units[n]
                s0 = SLOT - nb * P
                edge = ones[:, :] if j0 + nb == t + 1 else stick[:, (n - 1) % 2, SLOT - units[n - 1][4] * P][:, None]
                wait(dve, a_done[n % 2], (NU // 2) * p + n // 2)
                wait(dve, scan_done, NU * p + n)
                nc.vector.tensor_copy(stick[:, n % 2, SLOT:SLOT + 1], edge).then_inc(edge_set, 1)
                dve.wait_ge(keep_done, NU * p + n + 1)
                nc.vector.tensor_tensor_scan(stick[:, n % 2, s0:SLOT][:, ::-1], keep[:, n % 2, 0:nb * P][:, ::-1],
                                             keep[:, n % 2, 0:nb * P][:, ::-1],
                                             edge, ALU.mult, ALU.bypass).then_inc(scan_done, 1)

            def a_unit(p, n):
                nb = units[n][4]
                dve.wait_ge(z_read, NU * p + n + 1)
                dve.wait_ge(scan_done, NU * p + n + 1)
                dve.wait_ge(edge_set, NU * p + n + 1)
                nc.vector.tensor_tensor(a[:, n % 4, 0:nb * P], a[:, n % 4, 0:nb * P],
                                        stick[:, n % 2, SLOT - nb * P + 1:SLOT + 1], ALU.mult).then_inc(a_done[0], 1)

            def aT_part(p, n):
                p, n = at(p, n)
                gi, h, t, j0, nb = units[n]
                for f in range(fills[n], fills[n + 1]):
                    j = 4 * (f - fills[n])
                    nj = min(4, nb - j)
                    blocks, toks = slice(j0 + j, j0 + j + nj), slice((t % GT) * P, (t % GT + 1) * P)
                    dve.wait_ge(aT_hi_done, FILLS * p + f + 1)
                    nc.vector.tensor_tensor(aT_lo[:, gi % 2, blocks, toks], tr[:, f % 2, 0:nj, :],
                                            aT_hi[:, gi % 2, blocks, toks].bitcast(F32),
                                            ALU.subtract).then_inc(aT_lo_done, 1)

            def o_part(p, gi):
                p, gi = at(p, gi, NG)
                dve.wait_ge(o_low_done, NG * p + gi + 1)
                wait(dve, o_stored[gi % 2], (DMA * NG // 2) * p + DMA * (gi // 2))
                nc.vector.tensor_tensor(o_sb[:, gi % 2, :], o[0:HD, 0:GW], o_low[:, :], ALU.add).then_inc(o_done, 1)

            CHAIN = TAPS + 2

            def convolve(p, c):
                done = p * (CT * CHAIN) + c * CHAIN
                wait(dve, conv_chain, done)
                nc.vector.tensor_copy(cu[:, 0:HALO], halo[:, c, :]).then_inc(conv_chain, 1)
                dve.wait_ge(c_done, CT * p + c + 1)
                nc.vector.tensor_tensor(cu[:, HALO:HALO + BANK], proj[:, :], c_sb[:, :], ALU.mult).then_inc(cu_done, 1)
                dve.wait_ge(cu_done, CT * p + c + 1)
                dve.wait_ge(conv_chain, done + 1)
                wait(dve, y_done, CT * p + c)
                nc.vector.tensor_scalar(conv[:, :], cu[:, HALO:HALO + BANK], taps[:, c, TAPS - 1:TAPS], None,
                                        ALU.mult).then_inc(conv_chain, 1)
                for w in reversed(range(TAPS - 1)):
                    dve.wait_ge(conv_chain, done + TAPS - w)
                    nc.vector.scalar_tensor_tensor(out=conv[:, :], in0=cu[:, w:w + BANK], scalar=taps[:, c, w:w + 1],
                                                   in1=conv[:, :], op0=ALU.mult, op1=ALU.add).then_inc(conv_chain, 1)
                nc.vector.tensor_copy(halo[:, c, :], cu[:, BANK:BANK + HALO]).then_inc(conv_chain, 1)

            def body(p):
                for n in range(NU):
                    running_product(p, n)
                    if n % 2 == 0:
                        a_unit(p, n)
                    if n >= LAG or not isinstance(p, int):
                        aT_part(p, n - LAG)
                    q, b = at(p, n - LAG - 1)
                    if opens[b] and (n - LAG - 1 > 0 or not isinstance(p, int)):
                        o_part(q, units[b][0] - 1)
                    k = ends.get(n - 1, 0)
                    if k % 3 == 1:
                        dve.wait_ge(proj_full, NPROJ * p + k + 1)
                        convolve(p, k // 3)
                    if k % 3 == 2:
                        c = k // 3
                        dve.wait_ge(proj_full, NPROJ * p + k + 1)
                        dve.wait_ge(conv_chain, p * (CT * CHAIN) + (c + 1) * CHAIN)
                        wait(dve, y_stored, DMA * CT * p + DMA * c)
                        nc.vector.tensor_tensor(y[:, :], proj[:, :], conv[:, :], ALU.mult).then_inc(y_done, 1)

            pairs(dve, body)
            for n in range(NU - LAG, NU):
                aT_part(PAIRS - 1, n)
                if opens[n - 1]:
                    o_part(PAIRS - 1, units[n - 1][0] - 1)
            o_part(PAIRS - 1, NG - 1)

        @block.gpsimd
        def _(pool):
            def a_unit(p, n):
                nb = units[n][4]
                pool.wait_ge(z_read, NU * p + n + 1)
                pool.wait_ge(edge_set, NU * p + n + 1)
                pool.wait_ge(scan_done, NU * p + n + 1)
                nc.gpsimd.tensor_tensor(a[:, n % 4, 0:nb * P], a[:, n % 4, 0:nb * P],
                                        stick[:, n % 2, SLOT - nb * P + 1:SLOT + 1], ALU.mult).then_inc(a_done[1], 1)

            def w_split(p, k):
                pool.wait_ge(w_hi_done, NPROJ * p + k + 1)
                nc.gpsimd.tensor_tensor(w_lo[:, k % 2, :, :], w_stage[:, :, :], w_hi[:, k % 2, :, :].bitcast(F32),
                                        ALU.subtract).then_inc(w_lo_done, 1)

            def body(p):
                for n in range(NU):
                    if n % 2 == 1:
                        a_unit(p, n)
                    if n == 1:
                        w_split(p, 0)
                    if n in starts and starts[n] + 1 < NPROJ:
                        w_split(p, starts[n] + 1)

            pairs(pool, body)

        @block.tensor
        def _(pe):
            def scores(p, n):
                gi, h, t, j0, nb = units[n]
                g = gi // 2
                if opens[n]:
                    if g == 0:
                        pe.wait_ge(k_in[h], 2 * DMA * p + 2 * DMA)
                    pe.wait_ge(q_in[h][g % 2], 4 * DMA * (NG // 4) * p + 4 * DMA * (g // 2 + 1))
                wait(pe, z_read, NU * p + n - 1)
                tile = slice((t % GT) * P, (t % GT + 1) * P)
                for b0 in range(0, nb * P, BANK):
                    b1 = min(nb * P, b0 + BANK)
                    diagonal = j0 + b1 // P == t + 1
                    out, keys = z[:, n % 2, b0:b1], slice(j0 * P + b0, j0 * P + b1)
                    nc.tensor.matmul(out, q_hh[:, h, g % 2, tile], k_st[:, h, keys], start=True, stop=False)
                    last = nc.tensor.matmul(out, q_ll[:, h, g % 2, tile], k_st[:, h, keys],
                                            start=False, stop=not diagonal)
                    if diagonal:
                        last = nc.tensor.matmul(z[:, n % 2, b1 - P:b1], cst["ident_bf"][:, :], cst["mask_bf"][:, :],
                                                start=False, stop=True)
                last.then_inc(z_full, 1)

            def transposes(p, n):
                p, n = at(p, n)
                gi, h, t, j0, nb = units[n]
                pe.wait_ge(a_done[n % 2], (NU // 2) * p + n // 2 + 1)
                for f in range(fills[n], fills[n + 1]):
                    wait(pe, aT_lo_done, FILLS * p + f - 1)
                    j = 4 * (f - fills[n])
                    for i in range(min(4, nb - j)):
                        last = nc.tensor.transpose(tr[:, f % 2, i, :], a[:, n % 4, (j + i) * P:(j + i + 1) * P],
                                                   cst["ident"][:, :])
                    last.then_inc(tr_full, 1)

            def a_times_v(p, gi):
                p, gi = at(p, gi, NG)
                h, g = gi % 2, gi // 2
                blocks = GT * (g + 1)
                pe.wait_ge(aT_lo_done, FILLS * p + fills[group_units[gi + 1]])
                if g == 0:
                    pe.wait_ge(v_in[h], DMA * p + DMA)
                wait(pe, o_done, NG * p + gi)
                for j in range(blocks):
                    c = max(0, j - GT * g) * P
                    for part in (aT_hi, aT_lo):
                        last = nc.tensor.matmul(o[:, c:GW], v_st[:, h, j, :], part[:, gi % 2, j, c:GW],
                                                start=j == 0 and part is aT_hi,
                                                stop=j == blocks - 1 and part is aT_lo)
                last.then_inc(o_full, 1)

            def project_step(p, k, i):
                if k == 0:
                    pe.wait_ge(hT_in[i], 2 * DMA * p + 2 * DMA)
                if i == 0:
                    pe.wait_ge(w_lo_done, NPROJ * p + k + 1)
                    if k % 3 == 0:
                        wait(pe, y_done, CT * p + k // 3)
                    elif k % 3 == 1:
                        pe.wait_ge(c_done, CT * p + k // 3 + 1)
                    else:
                        pe.wait_ge(cu_done, CT * p + k // 3 + 1)
                last = matmul3(nc, proj[:, :], w_hi[:, k % 2, i, :], w_lo[:, k % 2, i, :],
                               hT_hi[:, i, :], hT_lo[:, i, :], i == 0, i == KT - 1)
                if i == KT - 1:
                    last.then_inc(proj_full, 1)
                elif k == NPROJ - 1:
                    last.then_inc(hT_used, 1)

            def body(p):
                for n in range(NU):
                    scores(p, n)
                    if n >= LAG or not isinstance(p, int):
                        transposes(p, n - LAG)
                        q, b = at(p, n - LAG)
                        if opens[b] and (n > LAG or not isinstance(p, int)):
                            a_times_v(q, units[b][0] - 1)
                    for k, i in steps[n]:
                        project_step(p, k, i)

            pairs(pe, body)
            for n in range(NU - LAG, NU):
                transposes(PAIRS - 1, n)
                if opens[n]:
                    a_times_v(PAIRS - 1, units[n][0] - 1)
            a_times_v(PAIRS - 1, NG - 1)


def mix_stage(nc, cst, G, acc, h2T_hi, h2T_lo, x, norm_ffn, w_out, mixT_dram):
    S, D = x.shape
    TOK = acc.shape[1] * P
    TILES = TOK // P
    KT = D // P
    NH = D // BANK
    NB = KT // 4
    with ExitStack() as stack:
        m = Pool_(nc, stack, f"mix{G}_")
        w_stage = m.sb("w_stage", [P, 2, D])
        w_hi, w_lo = m.sb("w_hi", [P, KT, D], F32R), m.sb("w_lo", [P, KT, D], F32R)
        mix_t = m.sb("mix_t", [P, 2, KT, P])
        mix_hi, mix_lo = m.sb("mix_hi", [P, 2, KT, P], F32R), m.sb("mix_lo", [P, 2, KT, P], F32R)
        gain = m.sb("gain", [P, D])
        square = m.sb("square", [P, D], BF16)
        ss, msq, rstd = m.sb("ss", [P, 1]), m.sb("msq", [P, 1]), m.sb("rstd", [P, 1])
        xn = m.sb("xn", [P, D])
        proj = m.ps("proj", [P, 2, NH, BANK])
        tr = m.ps("tr", [P, 2, 4, P])

        gain_in, acc_in, mix_in = m.sem("gain_in"), m.sem("acc_in"), [m.sem("mix_in0"), m.sem("mix_in1")]
        w_in_sem = [m.sem("w_in0"), m.sem("w_in1")]
        w_hi_done, w_lo_done, mix_hi_done, mix_lo_done = (
            m.sem(n) for n in ("w_hi_done", "w_lo_done", "mix_hi_done", "mix_lo_done"))
        proj_full, acc_done, ss_done, msq_done, rstd_done, xn_done = (
            m.sem(n) for n in ("proj_full", "acc_done", "ss_done", "msq_done", "rstd_done", "xn_done"))
        tr_full, hT_hi_done, hT_lo_done = m.sem("tr_full"), m.sem("hT_hi_done"), m.sem("hT_lo_done")
        block = m.block()

        def tiles(eng, step):
            step(0, 0, first=True)
            step(1, 1)
            step(2, 0)
            with eng.Fori(1, (TILES - 2) // 2) as i:
                step(2 * i + 1, 1)
                step(2 * i + 2, 0)
            step(TILES - 1, (TILES - 1) % 2, last=True)

        @block.sync
        def _(sp):
            def load(t, b):
                wait(sp, mix_lo_done, t - 1)
                sp.dma_start(mix_t[:, b, :, :], mixT_dram.rearrange("(k p) t -> p k t", p=P)
                             [:, :, bass.ds(G * TOK + t * P, P)]).then_inc(mix_in[b], DMA)

            load(0, 0)
            sp.dma_start(gain[:, :], norm_ffn.partition_broadcast(P)).then_inc(gain_in, DMA)
            for k in range(KT):
                wait(sp, w_lo_done, k - 1)
                sp.dma_start(w_stage[:, k % 2, :], w_out[k * P:(k + 1) * P, :]).then_inc(w_in_sem[k % 2], DMA)
                if k == 1:
                    sp.dma_start(acc[:, :, :], x[G * TOK:(G + 1) * TOK, :].rearrange("(t p) d -> p t d", p=P)
                                 ).then_inc(acc_in, DMA)

            def step(t, b, first=False, last=False):
                if not last:
                    load(t + 1, 1 - b)

            tiles(sp, step)

        @block.gpsimd
        def _(pool):
            with pool.Fori(0, TILES) as t:
                pool.wait_ge(ss_done, t + 1)
                pool.wait_ge(xn_done, t)
                nc.gpsimd.tensor_tensor(msq[:, :], ss[:, :], cst["eps"][:, 0:1], ALU.add).then_inc(msq_done, 1)
                pool.wait_ge(msq_done, t + 1)
                nc.gpsimd.tensor_tensor(rstd[:, :], msq[:, :], cst["minus_half"][:, 0:1],
                                        ALU.pow).then_inc(rstd_done, 1)

        @block.scalar
        def _(act):
            def mix_split(t, b):
                act.wait_ge(mix_in[b], (t - b) * (DMA // 2) + DMA)
                wait(act, proj_full, NH * (t - 1))
                nc.scalar.activation(mix_hi[:, b, :, :], mix_t[:, b, :, :], ACT.Copy).then_inc(mix_hi_done, 1)

            def hT_part(t, n):
                act.wait_ge(tr_full, NB * t + n + 1)
                nc.scalar.activation(h2T_hi[:, 4 * n:4 * n + 4, bass.ds(t * P, P)], tr[:, n % 2, :, :],
                                     ACT.Copy).then_inc(hT_hi_done, 1)

            mix_split(0, 0)
            for k in range(KT):
                act.wait_ge(w_in_sem[k % 2], DMA * (k // 2 + 1))
                nc.scalar.activation(w_hi[:, k, :], w_stage[:, k % 2, :], ACT.Copy).then_inc(w_hi_done, 1)

            def step(t, b, first=False, last=False):
                if not last:
                    mix_split(t + 1, 1 - b)
                if not first:
                    for n in range(NB):
                        hT_part(t - 1, n)
                act.wait_ge(acc_done, NH * (t + 1))
                wait(act, msq_done, t)
                wait(act, ss_done, t)
                nc.scalar.activation(square[:, :], acc[:, t, :], ACT.Square, scale=D ** -0.5,
                                     accum_out=ss[:, :]).then_inc(ss_done, 1)

            tiles(act, step)
            for n in range(NB):
                hT_part(TILES - 1, n)

        @block.vector
        def _(dve):
            def mix_split(t, b):
                dve.wait_ge(mix_hi_done, t + 1)
                nc.vector.tensor_tensor(mix_lo[:, b, :, :], mix_t[:, b, :, :], mix_hi[:, b, :, :].bitcast(F32),
                                        ALU.subtract).then_inc(mix_lo_done, 1)

            def hT_part(t, n):
                dve.wait_ge(hT_hi_done, NB * t + n + 1)
                nc.vector.tensor_tensor(h2T_lo[:, 4 * n:4 * n + 4, bass.ds(t * P, P)], tr[:, n % 2, :, :],
                                        h2T_hi[:, 4 * n:4 * n + 4, bass.ds(t * P, P)].bitcast(F32),
                                        ALU.subtract).then_inc(hT_lo_done, 1)

            mix_split(0, 0)
            for k in range(KT):
                dve.wait_ge(w_hi_done, k + 1)
                nc.vector.tensor_tensor(w_lo[:, k, :], w_stage[:, k % 2, :], w_hi[:, k, :].bitcast(F32),
                                        ALU.subtract).then_inc(w_lo_done, 1)
            dve.wait_ge(acc_in, DMA)
            dve.wait_ge(gain_in, DMA)

            def step(t, b, first=False, last=False):
                if not last:
                    mix_split(t + 1, 1 - b)
                if not first:
                    for n in range(NB):
                        hT_part(t - 1, n)
                for n in range(NH):
                    dve.wait_ge(proj_full, NH * t + n + 1)
                    nc.vector.tensor_tensor(acc[:, t, n * BANK:(n + 1) * BANK], acc[:, t, n * BANK:(n + 1) * BANK],
                                            proj[:, b, n, :], ALU.add).then_inc(acc_done, 1)
                dve.wait_ge(rstd_done, t + 1)
                wait(dve, tr_full, NB * t)
                dve.wait_ge(acc_done, NH * (t + 1))
                nc.vector.scalar_tensor_tensor(out=xn[:, :], in0=acc[:, t, :], scalar=rstd[:, 0:1], in1=gain[:, :],
                                               op0=ALU.mult, op1=ALU.mult).then_inc(xn_done, 1)

            tiles(dve, step)
            for n in range(NB):
                hT_part(TILES - 1, n)

        @block.tensor
        def _(pe):
            pe.wait_ge(w_lo_done, KT)

            def transposes(t):
                pe.wait_ge(xn_done, t + 1)
                for n in range(NB):
                    wait(pe, hT_lo_done, NB * t)
                    for j in range(4):
                        k = 4 * n + j
                        last = nc.tensor.transpose(tr[:, n % 2, j, :], xn[:, k * P:(k + 1) * P], cst["ident"][:, :])
                    last.then_inc(tr_full, 1)

            def step(t, b, first=False, last=False):
                pe.wait_ge(mix_lo_done, t + 1)
                wait(pe, acc_done, NH * (t - 1))
                for n in range(NH):
                    cols = slice(n * BANK, (n + 1) * BANK)
                    for k in range(KT):
                        last_mm = matmul3(nc, proj[:, b, n, :], mix_hi[:, b, k, :], mix_lo[:, b, k, :],
                                          w_hi[:, k, cols], w_lo[:, k, cols], k == 0, k == KT - 1)
                    last_mm.then_inc(proj_full, 1)
                    if n == 0 and not first:
                        transposes(t - 1)

            tiles(pe, step)
            transposes(TILES - 1)


def ffn_stage(nc, cst, G, acc, h2T_hi, h2T_lo, w_gate, w_up, w_down, out):
    D, FF = w_gate.shape
    KT = D // P
    TOK = acc.shape[1] * P
    TILES = TOK // P
    NT = TOK // BANK
    NH = D // BANK
    CHUNKS = FF // P
    PER = TILES // (2 * NT)
    with ExitStack() as stack:
        m = Pool_(nc, stack, f"ffn{G}_")
        gu_stage, d_stage = m.sb("gu_stage", [P, 2, 2, KT, P]), m.sb("d_stage", [P, 2, D])
        gu_hi, gu_lo = m.sb("gu_hi", [P, 2, 2, KT, P], F32R), m.sb("gu_lo", [P, 2, 2, KT, P], F32R)
        d_hi, d_lo = m.sb("d_hi", [P, 2, D], F32R), m.sb("d_lo", [P, 2, D], F32R)
        silu = m.sb("silu", [P, 2, BANK])
        hid = m.sb("hid", [P, 2, BANK])
        hid_hi, hid_lo = m.sb("hid_hi", [P, 2, TOK], F32R), m.sb("hid_lo", [P, 2, TOK], F32R)
        gate, up = m.ps("gate", [P, 2, BANK]), m.ps("up", [P, 2, BANK])
        down = m.ps("down", [P, 2, NH, BANK])

        gu_in, d_in = [m.sem("gu_in0"), m.sem("gu_in1")], [m.sem("d_in0"), m.sem("d_in1")]
        gu_hi_done, gu_lo_done, d_hi_done, d_lo_done = (
            m.sem(n) for n in ("gu_hi_done", "gu_lo_done", "d_hi_done", "d_lo_done"))
        gate_full, up_full, silu_done, hid_done, hid_hi_done, hid_lo_done = (
            m.sem(n) for n in ("gate_full", "up_full", "silu_done", "hid_done", "hid_hi_done", "hid_lo_done"))
        down_full, acc_done, stored = m.sem("down_full"), m.sem("acc_done"), m.sem("stored")
        block = m.block()

        def chunks(eng, step):
            step(0, 0, first=True)
            step(1, 1)
            step(2, 0)
            with eng.Fori(1, (CHUNKS - 2) // 2) as i:
                step(2 * i + 1, 1)
                step(2 * i + 2, 0)
            step(CHUNKS - 1, (CHUNKS - 1) % 2, last=True)

        @block.sync
        def _(sp):
            def load_gu(c, b):
                wait(sp, gu_lo_done, c - 1)
                for j, w in enumerate((w_gate, w_up)):
                    sp.dma_start(gu_stage[:, b, j, :, :], w.rearrange("(k p) f -> p k f", p=P)
                                 [:, :, bass.ds(c * P, P)]).then_inc(gu_in[b], DMA)

            def load_d(c, b):
                wait(sp, d_lo_done, c - 1)
                sp.dma_start(d_stage[:, b, :], w_down[bass.ds(c * P, P), :]).then_inc(d_in[b], DMA)

            load_gu(0, 0)

            def step(c, b, first=False, last=False):
                if not last:
                    load_gu(c + 1, 1 - b)
                load_d(c, b)

            chunks(sp, step)
            for t in range(TILES):
                sp.wait_ge(acc_done, TILES * (CHUNKS - 1) + t + 1)
                sp.dma_start(out[G * TOK + t * P:G * TOK + (t + 1) * P, :], acc[:, t, :]).then_inc(stored, DMA)
            sp.wait_ge(stored, DMA * TILES)

        @block.scalar
        def _(act):
            def gu_split(c, b):
                act.wait_ge(gu_in[b], (c - b) * DMA + 2 * DMA)
                wait(act, up_full, NT * (c - 1))
                nc.scalar.activation(gu_hi[:, b, :, :, :], gu_stage[:, b, :, :, :], ACT.Copy).then_inc(gu_hi_done, 1)

            gu_split(0, 0)

            def step(c, b, first=False, last=False):
                for n in range(NT):
                    act.wait_ge(gate_full, NT * c + n + 1)
                    wait(act, hid_done, NT * (c - 1) + n + 1)
                    nc.scalar.activation(silu[:, n % 2, :], gate[:, n % 2, :], ACT.Silu).then_inc(silu_done, 1)
                    if n == 0 and not last:
                        gu_split(c + 1, 1 - b)
                    if n == 1:
                        act.wait_ge(d_in[b], (c - b) * (DMA // 2) + DMA)
                        wait(act, down_full, TILES * (c - 1))
                        nc.scalar.activation(d_hi[:, b, :], d_stage[:, b, :], ACT.Copy).then_inc(d_hi_done, 1)
                    act.wait_ge(hid_done, NT * c + n + 1)
                    wait(act, down_full, TILES * (c - 1))
                    nc.scalar.activation(hid_hi[:, b, n * BANK:(n + 1) * BANK], hid[:, n % 2, :],
                                         ACT.Copy).then_inc(hid_hi_done, 1)

            chunks(act, step)

        @block.vector
        def _(dve):
            def gu_split(c, b):
                dve.wait_ge(gu_hi_done, c + 1)
                nc.vector.tensor_tensor(gu_lo[:, b, :, :, :], gu_stage[:, b, :, :, :],
                                        gu_hi[:, b, :, :, :].bitcast(F32), ALU.subtract).then_inc(gu_lo_done, 1)

            gu_split(0, 0)

            def add_tiles(c, t0):
                for t in range(t0, t0 + PER):
                    dve.wait_ge(down_full, TILES * c + t + 1)
                    wait(dve, acc_done, TILES * (c - 1) + t + 1)
                    nc.vector.tensor_tensor(acc[:, t, :], acc[:, t, :],
                                            down[:, t % 2, :, :].rearrange("p h n -> p (h n)"),
                                            ALU.add).then_inc(acc_done, 1)

            def step(c, b, first=False, last=False):
                for n in range(NT):
                    if not first:
                        add_tiles(c - 1, 2 * n * PER)
                    dve.wait_ge(silu_done, NT * c + n + 1)
                    dve.wait_ge(up_full, NT * c + n + 1)
                    wait(dve, hid_lo_done, NT * (c - 1) + n + 1)
                    nc.vector.tensor_tensor(hid[:, n % 2, :], silu[:, n % 2, :], up[:, n % 2, :],
                                            ALU.mult).then_inc(hid_done, 1)
                    if n == 0 and not last:
                        gu_split(c + 1, 1 - b)
                    if not first:
                        add_tiles(c - 1, (2 * n + 1) * PER)
                    if n == 1:
                        dve.wait_ge(d_hi_done, c + 1)
                        nc.vector.tensor_tensor(d_lo[:, b, :], d_stage[:, b, :], d_hi[:, b, :].bitcast(F32),
                                                ALU.subtract).then_inc(d_lo_done, 1)
                    dve.wait_ge(hid_hi_done, NT * c + n + 1)
                    nc.vector.tensor_tensor(hid_lo[:, b, n * BANK:(n + 1) * BANK], hid[:, n % 2, :],
                                            hid_hi[:, b, n * BANK:(n + 1) * BANK].bitcast(F32),
                                            ALU.subtract).then_inc(hid_lo_done, 1)

            chunks(dve, step)
            for part in range(2 * NT):
                add_tiles(CHUNKS - 1, part * PER)

        @block.tensor
        def _(pe):
            def hidden(c, b, n, j, bank, full):
                for k in range(KT):
                    toks = slice(n * BANK, (n + 1) * BANK)
                    last = matmul3(nc, bank[:, n % 2, :], gu_hi[:, b, j, k, :], gu_lo[:, b, j, k, :],
                                   h2T_hi[:, k, toks], h2T_lo[:, k, toks], k == 0, k == KT - 1)
                last.then_inc(full, 1)

            def down_tiles(c, b, t0):
                pe.wait_ge(hid_lo_done, NT * (c + 1))
                pe.wait_ge(d_lo_done, c + 1)
                for t in range(t0, t0 + PER):
                    wait(pe, acc_done, TILES * c + t - 1)
                    for h in range(NH):
                        toks, cols = slice(t * P, (t + 1) * P), slice(h * BANK, (h + 1) * BANK)
                        last = matmul3(nc, down[:, t % 2, h, :], hid_hi[:, b, toks], hid_lo[:, b, toks],
                                       d_hi[:, b, cols], d_lo[:, b, cols], True, True)
                    last.then_inc(down_full, 1)

            def step(c, b, first=False, last=False):
                pe.wait_ge(gu_lo_done, c + 1)
                for n in range(NT):
                    wait(pe, silu_done, NT * (c - 1) + n + 1)
                    hidden(c, b, n, 0, gate, gate_full)
                    if not first:
                        down_tiles(c - 1, 1 - b, 2 * n * PER)
                    wait(pe, hid_done, NT * (c - 1) + n + 1)
                    hidden(c, b, n, 1, up, up_full)
                    if not first:
                        down_tiles(c - 1, 1 - b, (2 * n + 1) * PER)

            chunks(pe, step)
            for part in range(2 * NT):
                down_tiles(CHUNKS - 1, (CHUNKS - 1) % 2, part * PER)


def decoder_layer(nc, x, norm_mix, w_in, q_norm, k_norm, conv_w, w_out, norm_ffn, w_gate, w_up, w_down, out):
    x, out = x[0, :, :], out[0, :, :]
    norm_mix, q_norm, k_norm, norm_ffn = norm_mix[0, :], q_norm[0, :], k_norm[0, :], norm_ffn[0, :]
    w_in, conv_w, w_out = w_in[0, :, :], conv_w[0, :, :], w_out[0, :, :]
    w_gate, w_up, w_down = w_gate[0, :, :], w_up[0, :, :], w_down[0, :, :]
    S, D = x.shape
    HD = q_norm.shape[0]
    CD = conv_w.shape[1]
    AD = D - CD
    HALVES = 2
    qk_hi_dram = nc.dram_tensor("qk_hi", [2 * AD, S], F32).ap()
    qk_lo_dram = nc.dram_tensor("qk_lo", [2 * AD, S], F32).ap()
    v_dram = nc.dram_tensor("v_rows", [S, AD // HD, 2 * HD], F32).ap()
    hT_hi_dram = nc.dram_tensor("hT_hi", [D, S], F32).ap()
    hT_lo_dram = nc.dram_tensor("hT_lo", [D, S], F32).ap()
    mixT_dram = nc.dram_tensor("mixT", [D, S], F32).ap()
    with ExitStack() as stack:
        m = Pool_(nc, stack, "all_")
        cst = {
            "ident": m.sb("ident", [P, P]),
            "ident_bf": m.sb("ident_bf", [P, P], BF16),
            "mask_bf": m.sb("mask_bf", [P, P], BF16),
            "minus_half": m.sb("minus_half", [P, 2 * AD // HD]),
            "eps": m.sb("eps", [P, 2 * AD // HD]),
        }
        constants(nc, cst)
        qkv_stage(nc, cst, x, norm_mix, w_in, q_norm, k_norm, hT_hi_dram, hT_lo_dram, qk_hi_dram, qk_lo_dram, v_dram)
        attend_conv_stage(nc, cst, hT_hi_dram, hT_lo_dram, w_in, conv_w, qk_hi_dram, qk_lo_dram, v_dram, mixT_dram, HD)
        acc = m.sb("acc", [P, S // HALVES // P, D])
        h2T_hi = m.sb("h2T_hi", [P, D // P, S // HALVES], F32R)
        h2T_lo = m.sb("h2T_lo", [P, D // P, S // HALVES], F32R)
        for G in range(HALVES):
            mix_stage(nc, cst, G, acc, h2T_hi, h2T_lo, x, norm_ffn, w_out, mixT_dram)
            ffn_stage(nc, cst, G, acc, h2T_hi, h2T_lo, w_gate, w_up, w_down, out)


_INS = ["x", "norm_mix", "w_in", "q_norm", "k_norm", "conv_w", "w_out", "norm_ffn", "w_gate", "w_up", "w_down"]


def kernel(**inputs):
    import numpy as np
    import concourse.bacc as bacc
    from concourse.bass_utils import run_bass_kernel_spmd

    nc = bacc.Bacc("TRN2", target_bir_lowering=False, num_devices=1)
    arrays, args = {}, []
    for name in _INS:
        a = np.ascontiguousarray(inputs[name])
        arrays[f"in_{name}"] = a
        args.append(nc.dram_tensor(f"in_{name}", a.shape, mybir.dt.from_np(a.dtype), kind="ExternalInput").ap())
    out = nc.dram_tensor("out", inputs["x"].shape, F32, kind="ExternalOutput").ap()
    decoder_layer(nc, *args, out)
    r = run_bass_kernel_spmd(nc, [arrays], core_ids=[0])
    return r.results[0]["out"]
```
